# Optimizing a Trainium2 kernel written in Bass

```python
import math
import jax, jax.numpy as jnp
from jax import lax
import numpy as np

"""Two layers of a bidirectional hybrid encoder trunk.

Per layer (sandwich RMSNorm around every sub-layer):
  x += 0.5 * post(SwiGLU(pre(x)))                       macaron half-step FFN 1
  u  = pre(x); P = u @ w_in  (one combined projection, columns split over head groups)
       A: 2-D neighbourhood attention (6 heads)   B: bidirectional Hyena order 2 (256 ch)
       C: LongNet dilated sliding-window attention (6 heads, 3 dilations, T5 bias)
  x += post(concat(groupnorm(A), groupnorm(B), groupnorm(C)) @ w_out)
  x += post(CrossAttn(pre(x), norm(mem)))               4-head memory cross-attention
  x += 0.5 * post(SwiGLU(pre(x)))                       macaron half-step FFN 2
Inputs: x (BATCH, SEQ, D_MODEL), mem (BATCH, 256, D_MODEL), per-layer stacked weights.
Output: (BATCH, SEQ, D_MODEL).
"""

D_MODEL = 1024
BATCH = 1
SEQ = 512
DEPTH = 2

GRID_W = 64
MEM_LEN = 256
HEAD_DIM = 64
NA_HEADS = 6
NA_WIDTH = NA_HEADS * HEAD_DIM
HY_WIDTH = 256
DIL_HEADS = 6
DIL_WIDTH = DIL_HEADS * HEAD_DIM
MIX_WIDTH = NA_WIDTH + HY_WIDTH + DIL_WIDTH
IN_COLS = 3 * MIX_WIDTH
NA_ROWS = 8
NA_COLS = 16
HY_SHORT = 3
HY_BANDS = 16
HY_EMB = 2 * HY_BANDS + 1
HY_FILTER_W = 64
HY_SHORT_DECAY_PCT = 0.3
HY_LONG_DECAY_PCT = 1.5
HY_TARGET = 1e-2
DIL_CONFIGS = ((128, 1), (512, 4), (2048, 16))
T5_BUCKETS = 32
T5_MAX_DIST = 1024
XA_HEADS = 4
XA_HEAD_DIM = D_MODEL // XA_HEADS
FFN_HIDDEN = 2816
RMS_EPS = 1e-6
NEG_INF = -1e30
FFN1_PRE, FFN1_POST, MIX_PRE, MIX_GROUP, MIX_POST, XA_PRE, XA_MEM, XA_POST, FFN2_PRE, FFN2_POST = range(10)
N_NORMS = 10

kernel_name = "hybrid_natten_hyena_dilated_encoder"

def rms_norm(x, g):
    xf = x.astype(jnp.float32)
    y = xf * lax.rsqrt(jnp.mean(xf * xf, axis=-1, keepdims=True) + RMS_EPS)
    return (y * g.astype(jnp.float32)).astype(x.dtype)

def swiglu(x, w_in, w_out):
    gate, up = jnp.split(x @ w_in, 2, axis=-1)
    return (jax.nn.silu(gate) * up) @ w_out

def t5_bucket(rel):
    half = T5_BUCKETS // 2
    exact = half // 2
    n = np.abs(rel)
    far = exact + (np.log(np.maximum(n, 1) / exact) / math.log(T5_MAX_DIST / exact) * (half - exact)).astype(np.int32)
    far = np.minimum(far, half - 1)
    return (np.where(rel > 0, half, 0) + np.where(n < exact, n, far)).astype(np.int32)

def neighbourhood_attn(q, k, v, rpb):
    B, L, H, hd = q.shape
    rows = L // GRID_W
    wr = min(NA_ROWS, rows)
    qg = q.reshape(B, rows, GRID_W, H, hd)
    kg = k.reshape(B, rows, GRID_W, H, hd)
    vg = v.reshape(B, rows, GRID_W, H, hd)
    col = np.arange(GRID_W)
    cs = np.clip(col - NA_COLS // 2, 0, GRID_W - NA_COLS)
    col_idx = cs[:, None] + np.arange(NA_COLS)[None, :]
    col_off = col_idx - col[:, None] + NA_COLS - 1

    def row_step(r):
        rs = jnp.clip(r - wr // 2, 0, rows - wr)
        kr = lax.dynamic_slice_in_dim(kg, rs, wr, axis=1)
        vr = lax.dynamic_slice_in_dim(vg, rs, wr, axis=1)
        kn = kr[:, :, col_idx]
        vn = vr[:, :, col_idx]
        qr = lax.dynamic_index_in_dim(qg, r, axis=1, keepdims=False)
        s = jnp.einsum('bqhd,bwqkhd->bhqwk', qr, kn).astype(jnp.float32)
        row_off = rs + jnp.arange(wr) - r + NA_ROWS - 1
        bias = rpb[:, row_off[None, :, None], col_off[:, None, :]]
        s = s + bias.astype(jnp.float32)[None]
        p = jax.nn.softmax(s.reshape(B, H, GRID_W, wr * NA_COLS), axis=-1)
        p = p.reshape(B, H, GRID_W, wr, NA_COLS).astype(v.dtype)
        return jnp.einsum('bhqwk,bwqkhd->bqhd', p, vn)

    out = lax.map(row_step, jnp.arange(rows))
    return out.transpose(1, 0, 2, 3, 4).reshape(B, L, H, hd)

def dilated_attn(q, k, v, dil, half, t5_table):
    B, L, H, hd = q.shape
    M = L // dil
    blk = half
    nb = -(-M // blk)
    Mp = nb * blk

    def classes(t):
        return t.reshape(B, M, dil, H, hd).transpose(0, 2, 1, 3, 4)

    qb = jnp.pad(classes(q), ((0, 0), (0, 0), (0, Mp - M), (0, 0), (0, 0))).reshape(B, dil, nb, blk, H, hd)

    def key_windows(t):
        tp = jnp.pad(classes(t), ((0, 0), (0, 0), (blk, Mp - M + blk), (0, 0), (0, 0)))
        tp = tp.reshape(B, dil, nb + 2, blk, H, hd)
        return jnp.concatenate([tp[:, :, :-2], tp[:, :, 1:-1], tp[:, :, 2:]], axis=3)

    kw = key_windows(k)
    vw = key_windows(v)
    rel = np.arange(3 * blk)[None, :] - blk - np.arange(blk)[:, None]
    bias = t5_table[t5_bucket(dil * rel)].transpose(2, 0, 1).astype(jnp.float32)
    key_idx = np.arange(nb)[:, None] * blk - blk + np.arange(3 * blk)[None, :]
    valid = (np.abs(rel) <= half)[None] & ((key_idx >= 0) & (key_idx < M))[:, None, :]
    s = jnp.einsum('bgnqhd,bgnkhd->bghnqk', qb, kw).astype(jnp.float32) + bias[None, None, :, None]
    s = jnp.where(valid[None, None, None], s, NEG_INF)
    m = jnp.max(s, axis=-1, keepdims=True)
    p = jnp.exp(s - m)
    den = jnp.sum(p, axis=-1, keepdims=True)
    o = jnp.einsum('bghnqk,bgnkhd->bgnqhd', (p / den).astype(v.dtype), vw)
    lse = (m + jnp.log(den))[..., 0]
    o = o.reshape(B, dil, Mp, H, hd)[:, :, :M].transpose(0, 2, 1, 3, 4).reshape(B, L, H, hd)
    lse = lse.transpose(0, 1, 3, 4, 2).reshape(B, dil, Mp, H)[:, :, :M].transpose(0, 2, 1, 3).reshape(B, L, H)
    return o, lse

def dilated_mixer(q, k, v, t5_table):
    outs, lses = [], []
    for window, dil in DIL_CONFIGS:
        o, lse = dilated_attn(q, k, v, dil, window // (2 * dil), t5_table)
        outs.append(o)
        lses.append(lse)
    alpha = jax.nn.softmax(jnp.stack(lses), axis=0)
    return jnp.einsum('cblh,cblhd->blhd', alpha.astype(q.dtype), jnp.stack(outs))

def short_conv(u, w, b):
    up = jnp.pad(u, ((0, 0), (1, 1), (0, 0)))
    return up[:, :-2] * w[0] + up[:, 1:-1] * w[1] + up[:, 2:] * w[2] + b

def hyena_filters(L, w1, b1, w2, b2, w3, b3, w4, freq, decay):
    f32 = jnp.float32
    t = jnp.linspace(0.0, 1.0, L, dtype=f32)[:, None]
    bands = jnp.linspace(1e-4, HY_BANDS - 1, HY_BANDS, dtype=f32)[None, :]
    ang = (2.0 * math.pi / L) * jnp.arange(L, dtype=f32)[:, None] * bands
    z = jnp.concatenate([t, jnp.cos(ang), -jnp.sin(ang)], axis=-1)
    fr = freq.astype(f32)
    h = jnp.sin(fr * (z @ w1.astype(f32) + b1.astype(f32)))
    h = jnp.sin(fr * (h @ w2.astype(f32) + b2.astype(f32)))
    h = jnp.sin(fr * (h @ w3.astype(f32) + b3.astype(f32)))
    h = h @ w4.astype(f32)
    return h * jnp.exp(-t * jnp.abs(decay.astype(f32)))

def bidir_long_conv(z, h_fwd, h_bwd):
    L, C = h_fwd.shape
    filt = jnp.concatenate([h_fwd, jnp.zeros((1, C), h_fwd.dtype), h_bwd[:0:-1]], axis=0)
    zf = jnp.fft.rfft(z, n=2 * L, axis=1)
    ff = jnp.fft.rfft(filt, axis=0)
    return jnp.fft.irfft(zf * ff[None], n=2 * L, axis=1)[:, :L]

def hyena_mixer(p, conv_w, conv_b, w1, b1, w2, b2, w3, b3, w4, freq, decay, skip):
    L = p.shape[1]
    uc = short_conv(p, conv_w, conv_b)
    v, x1, x0 = jnp.split(uc, 3, axis=-1)
    h = hyena_filters(L, w1, b1, w2, b2, w3, b3, w4, freq, decay)
    z = (x1 * v).astype(jnp.float32)
    y = bidir_long_conv(z, h[:, :HY_WIDTH], h[:, HY_WIDTH:]) + skip.astype(jnp.float32) * z
    return (x0.astype(jnp.float32) * y).astype(p.dtype)

def memory_cross_attn(h, m, wq, wkv, wo):
    B, L, _ = h.shape
    S = m.shape[1]
    q = (h @ wq).reshape(B, L, XA_HEADS, XA_HEAD_DIM) * XA_HEAD_DIM ** -0.5
    kv = (m @ wkv).reshape(B, S, 2, XA_HEADS, XA_HEAD_DIM)
    s = jnp.einsum('blhd,bmhd->bhlm', q, kv[:, :, 0]).astype(jnp.float32)
    p = jax.nn.softmax(s, axis=-1).astype(h.dtype)
    o = jnp.einsum('bhlm,bmhd->blhd', p, kv[:, :, 1]).reshape(B, L, D_MODEL)
    return o @ wo

def setup_inputs(seed: int = 0) -> dict:
    key = jax.random.key(seed)
    ks = jax.random.split(key, 26)

    def nrm(k, shape, scale):
        return scale * jax.random.normal(k, shape, jnp.float32)

    base = jnp.abs(jnp.linspace(math.log(HY_TARGET) / HY_LONG_DECAY_PCT, math.log(HY_TARGET) / HY_SHORT_DECAY_PCT, HY_WIDTH, dtype=jnp.float32))
    decay = jnp.concatenate([base, base])[None, :] * (1.0 + nrm(ks[17], (DEPTH, 2 * HY_WIDTH), 0.05))
    return {
        'x': nrm(ks[0], (BATCH, SEQ, D_MODEL), 1.0),
        'mem': nrm(ks[1], (BATCH, MEM_LEN, D_MODEL), 1.0),
        'norm_g': 1.0 + nrm(ks[2], (DEPTH, N_NORMS, D_MODEL), 0.05),
        'w_in': nrm(ks[3], (DEPTH, D_MODEL, IN_COLS), D_MODEL ** -0.5),
        'w_out': nrm(ks[4], (DEPTH, MIX_WIDTH, D_MODEL), MIX_WIDTH ** -0.5),
        'na_rpb': nrm(ks[5], (DEPTH, NA_HEADS, 2 * NA_ROWS - 1, 2 * NA_COLS - 1), 0.1),
        't5_table': nrm(ks[6], (T5_BUCKETS, DIL_HEADS), 0.1),
        'hy_conv_w': nrm(ks[7], (DEPTH, HY_SHORT, 3 * HY_WIDTH), HY_SHORT ** -0.5),
        'hy_conv_b': nrm(ks[8], (DEPTH, 3 * HY_WIDTH), 0.01),
        'hy_f_w1': nrm(ks[9], (DEPTH, HY_EMB, HY_FILTER_W), HY_EMB ** -0.5),
        'hy_f_b1': nrm(ks[10], (DEPTH, HY_FILTER_W), 0.1),
        'hy_f_w2': nrm(ks[11], (DEPTH, HY_FILTER_W, HY_FILTER_W), HY_FILTER_W ** -0.5),
        'hy_f_b2': nrm(ks[12], (DEPTH, HY_FILTER_W), 0.1),
        'hy_f_w3': nrm(ks[13], (DEPTH, HY_FILTER_W, HY_FILTER_W), HY_FILTER_W ** -0.5),
        'hy_f_b3': nrm(ks[14], (DEPTH, HY_FILTER_W), 0.1),
        'hy_f_w4': nrm(ks[15], (DEPTH, HY_FILTER_W, 2 * HY_WIDTH), HY_FILTER_W ** -0.5),
        'hy_freq': 1.0 + nrm(ks[16], (DEPTH, HY_FILTER_W), 0.01),
        'hy_decay': decay,
        'hy_skip': nrm(ks[18], (DEPTH, HY_WIDTH), 1.0),
        'xa_wq': nrm(ks[19], (DEPTH, D_MODEL, D_MODEL), D_MODEL ** -0.5),
        'xa_wkv': nrm(ks[20], (DEPTH, D_MODEL, 2 * D_MODEL), D_MODEL ** -0.5),
        'xa_wo': nrm(ks[21], (DEPTH, D_MODEL, D_MODEL), D_MODEL ** -0.5),
        'ffn_w_in': nrm(ks[22], (DEPTH, 2, D_MODEL, 2 * FFN_HIDDEN), D_MODEL ** -0.5),
        'ffn_w_out': nrm(ks[23], (DEPTH, 2, FFN_HIDDEN, D_MODEL), FFN_HIDDEN ** -0.5),
    }

def reference(x, mem, norm_g, w_in, w_out, na_rpb, t5_table, hy_conv_w, hy_conv_b,
              hy_f_w1, hy_f_b1, hy_f_w2, hy_f_b2, hy_f_w3, hy_f_b3, hy_f_w4,
              hy_freq, hy_decay, hy_skip, xa_wq, xa_wkv, xa_wo, ffn_w_in, ffn_w_out):
    B, L, _ = x.shape
    scale = HEAD_DIM ** -0.5
    split_b = 3 * NA_WIDTH
    split_c = 3 * NA_WIDTH + 3 * HY_WIDTH
    for l in range(DEPTH):
        g = norm_g[l]
        x = x + 0.5 * rms_norm(swiglu(rms_norm(x, g[FFN1_PRE]), ffn_w_in[l, 0], ffn_w_out[l, 0]), g[FFN1_POST])

        u = rms_norm(x, g[MIX_PRE])
        proj = u @ w_in[l]
        pa, pb, pc = jnp.split(proj, [split_b, split_c], axis=-1)
        qa, ka, va = [t.reshape(B, L, NA_HEADS, HEAD_DIM) for t in jnp.split(pa, 3, axis=-1)]
        ya = neighbourhood_attn(qa * scale, ka, va, na_rpb[l]).reshape(B, L, NA_WIDTH)
        yb = hyena_mixer(pb, hy_conv_w[l], hy_conv_b[l], hy_f_w1[l], hy_f_b1[l], hy_f_w2[l], hy_f_b2[l],
                         hy_f_w3[l], hy_f_b3[l], hy_f_w4[l], hy_freq[l], hy_decay[l], hy_skip[l])
        qc, kc, vc = [t.reshape(B, L, DIL_HEADS, HEAD_DIM) for t in jnp.split(pc, 3, axis=-1)]
        yc = dilated_mixer(qc * scale, kc, vc, t5_table).reshape(B, L, DIL_WIDTH)
        gg = g[MIX_GROUP]
        y = jnp.concatenate([
            rms_norm(ya, gg[:NA_WIDTH]),
            rms_norm(yb, gg[NA_WIDTH:NA_WIDTH + HY_WIDTH]),
            rms_norm(yc, gg[NA_WIDTH + HY_WIDTH:]),
        ], axis=-1)
        x = x + rms_norm(y @ w_out[l], g[MIX_POST])

        xa = memory_cross_attn(rms_norm(x, g[XA_PRE]), rms_norm(mem, g[XA_MEM]), xa_wq[l], xa_wkv[l], xa_wo[l])
        x = x + rms_norm(xa, g[XA_POST])

        x = x + 0.5 * rms_norm(swiglu(rms_norm(x, g[FFN2_PRE]), ffn_w_in[l, 1], ffn_w_out[l, 1]), g[FFN2_POST])
    return x


_drawn_inputs = setup_inputs


def setup_inputs(seed=0):
    import zlib

    import numpy as np

    out = dict(_drawn_inputs(seed))
    spreads = {}
    factors = {'hy_conv_b': 6.375, 'hy_freq': 8.0}
    for name, (base, spread) in spreads.items():
        noise = np.random.default_rng([zlib.crc32(name.encode()), seed]).standard_normal(out[name].shape)
        drawn = base * np.exp(spread * noise) if base else spread * noise
        out[name] = __import__('jax').numpy.asarray(drawn.astype(out[name].dtype))
    for name, factor in factors.items():
        out[name] = (out[name] * factor).astype(out[name].dtype)
    return out
```

```python
from contextlib import ExitStack
import math

import numpy as np
import concourse.bass as bass
from concourse import mybir

ALU = mybir.AluOpType
ACT = mybir.ActivationFunctionType
F32 = mybir.dt.float32
F32R = mybir.dt.float32r
AX = mybir.AxisListType

P = 128
LAYERS = 2
D = 1024
T = 512
DT = D // P
MEM = 256
FF = 2816
FT = FF // P
FH = FT // 2
EPS = 1e-6
ROWS, COLS = 8, 64
NA_H = 6
WC, WR = 16, 8
C_H = 6
HYT = 2
FW = 64
EMB = 33
BIG = 1e30
STRIP = 7 * P

U_IN = (0, 124)
U_OUT = (44, 168)
U_HY, U_VA, U_VC, U_QA, U_KA, U_QC, U_KC = 60, 66, 69, 72, 75, 78, 81
U_WO, U_XQ, U_XK, U_XV, U_XO = 84, 92, 100, 108, 116
UNITS = 184
USED0, SPLIT0, EVAC0, X0 = 2, 4, 4, 1
IT_A, IT_C, IT_X, ITEMS = 0, 24, 48, 64
GR_A, GR_C, GR_X, GROUPS = 0, 4, 8, 16

TWO_PI_HI = 6.28125
TWO_PI_LO = 2 * math.pi - TWO_PI_HI
ROUND = 1.5 * 2.0 ** 23
PI_IN = 3.1415925
G0, CW0, CB0, SK0, NPAR = 0, 80, 98, 104, 106
PRE = (0, 2, 5, 8)
POST = (1, 4, 7, 9)
G_GROUP, G_MEM = 3, 6
NA_START = (0, 8, 24, 32)
NA_CHUNKS = (0, 8, 16, 24, 32, 40, 48)


def build(nc, x, mem, par, w_first, w_second, w_proj, rpb, t5, fw1, fw23, fw4, fvec, decay,
          k_emb, k_fwd, k_inv, k_time, k_namask, k_hot, k_lnn, k_eye, out):
    with ExitStack() as ctx:
        def sb(name, shape, dt=F32):
            return ctx.enter_context(nc.sbuf_tensor(name, shape, dt))

        def sem(name):
            return ctx.enter_context(nc.semaphore(name))

        bank = [ctx.enter_context(nc.psum_tensor(f"bank{i}", [P, 512], F32)) for i in range(8)]

        xT = sb("xT", [P, DT, T])
        raw = [sb(f"raw{i}", [P, FH * P]) for i in range(4)]
        wh = [sb(f"wh{i}", [P, FH * P], F32R) for i in range(2)]
        wl = [sb(f"wl{i}", [P, FH * P], F32R) for i in range(2)]
        rs = sb("rs", [P, T])
        rsq = sb("rsq", [P, T])
        rsp = sb("rsp", [P, T])
        rsm = sb("rsm", [P, MEM])
        tmp = [sb(f"tmp{i}", [P, T]) for i in range(6)]
        yb = [sb(f"yb{i}", [P, T]) for i in range(HYT)]
        ones = sb("ones", [P, P])
        eye = sb("eye", [P, P])
        epsc = sb("epsc", [P, 2])
        pr = sb("pr", [P, NPAR])
        negmax = sb("negmax", [P, ITEMS])
        den = sb("den", [P, ITEMS])
        rden = sb("rden", [P, ITEMS])
        gss = sb("gss", [P, 3, GROUPS])

        def overlay(*sets):
            return [over(s) for s in sets]

        base = nc.sbuf_base if not callable(nc.sbuf_base) else nc.sbuf_base()

        def place(parts):
            made = {}
            with ExitStack() as st:
                for name, shape, dt in parts:
                    made[name] = st.enter_context(nc.sbuf_tensor(name, shape, dt))
            return made

        yf = place([("yf", [P, DT, T], F32)])["yf"]
        uH = sb("uH", [P, DT, T], F32R)
        uL = sb("uL", [P, DT, T], F32R)
        hid = place([("hH", [P, FT * T], F32R), ("hL", [P, FT * T], F32R)])
        hH, hL = hid["hH"], hid["hL"]
        hy = place([
            ("p", [P, 6, T + 2], F32), ("uc", [P, 6, T], F32), ("fwd", [P, 2, 4, T], F32),
            ("inv", [P, 2, 4, T], F32), ("filt", [P, 2, 4, 256], F32), ("taps", [P, 4, 512], F32),
            ("even", [P, 4, 256], F32), ("zt", [P, 4, 256], F32), ("emb", [P, T], F32),
            ("w1", [P, FW], F32), ("w2", [P, FW], F32), ("w3", [P, FW], F32), ("w4", [P, 512], F32),
            ("fv", [P, 8], F32), ("tneg", [P, 4], F32)])
        at = place([
            ("qA", [P, 3, T], F32), ("kA", [P, 3, T], F32), ("vt", [P, 3, T], F32),
            ("VA", [P, 7, 384], F32), ("biasA", [P, 3, NA_H, 256], F32), ("qC", [P, 3, T], F32),
            ("kC", [P, 3, T], F32), ("VC", [P, 4, 384], F32), ("strip", [P, C_H, STRIP], F32)])
        xa = place([
            ("memT", [P, DT, MEM], F32), ("memH", [P, DT, MEM], F32R), ("memL", [P, DT, MEM], F32R),
            ("qX", [P, DT, T], F32), ("kX", [P, DT, MEM], F32), ("vX", [P, DT, MEM], F32),
            ("VX", [P, 2, D], F32), ("yx", [P, DT, T], F32)])
        st = place([("memS", [P, DT, MEM], F32), ("hot", [P, 1024], F32), ("lnn", [P, 1024], F32),
                    ("t5s", [P, 8], F32)])
        strip = at["strip"]
        rstrip = strip[:].rearrange("p h n -> p (h n)")[:, 0:NA_H * 384].rearrange(
            "p (h r c) -> p h r c", h=NA_H, r=WR)
        amask = strip[:].rearrange("p h n -> p (h n)")[:, NA_H * 384:NA_H * 384 + 768].rearrange(
            "p (y n) -> p y n", y=3)
        scratch = nc.dram_tensor("bias_of_distance", (C_H, 1024), F32, kind="Internal").ap()
        region = ctx.enter_context(nc.sbuf_tensor("region", [P, 2 * FT * T], F32))
        assert region is not None
        on = sb("on", [P, T])

        params_loaded = sem("params_loaded")
        setup_loaded = sem("setup_loaded")
        x_loaded = sem("x_loaded")
        landed = [sem(f"landed{i}") for i in range(4)]
        high_ready = sem("high_ready")
        split_ready = sem("split_ready")
        unit_done = sem("unit_done")
        evac = sem("evac")
        const_set = sem("const_set")
        x_ready = sem("x_ready")
        uh_ready = sem("uh_ready")
        u_ready = sem("u_ready")
        presq = sem("presq")
        presum = sem("presum")
        preroot = sem("preroot")
        rs_ready = sem("rs_ready")
        rsq_ready = sem("rsq_ready")
        postsq = sem("postsq")
        postacc = sem("postacc")
        postsum = sem("postsum")
        postroot = sem("postroot")
        rsp_ready = sem("rsp_ready")
        y_scaled = sem("y_scaled")
        gate_scaled = sem("gate_scaled")
        silu_ready = sem("silu_ready")
        hid_ready = sem("hid_ready")
        hidh_ready = sem("hidh_ready")
        hid_split = sem("hid_split")
        hy_loaded = sem("hy_loaded")
        pad_zero = sem("pad_zero")
        conv = sem("conv")
        z_ready = sem("z_ready")
        f_mm = sem("f_mm")
        f_arg = sem("f_arg")
        f_red = sem("f_red")
        f_sin = sem("f_sin")
        f_bias = sem("f_bias")
        taps_mm = sem("taps_mm")
        absd = sem("absd")
        window = sem("window")
        taps_ready = sem("taps_ready")
        filt_mm = sem("filt_mm")
        filt_ready = sem("filt_ready")
        zt_mm = sem("zt_mm")
        zt_ready = sem("zt_ready")
        z_mm = sem("z_mm")
        prod = sem("prod")
        y_mm = sem("y_mm")
        hyout = sem("hyout")
        hysq = sem("hysq")
        hysum = sem("hysum")
        hyroot = sem("hyroot")
        ybh = sem("ybh")
        m_ready = sem("m_ready")
        strips_loaded = sem("strips_loaded")
        bias_ready = sem("bias_ready")
        c_strip_loaded = sem("c_strip_loaded")
        vt_mm = sem("vt_mm")
        vt_out = sem("vt_out")
        score_mm = sem("score_mm")
        biased = sem("biased")
        prob_ready = sem("prob_ready")
        pt_mm = sem("pt_mm")
        pt_ready = sem("pt_ready")
        pv_mm = sem("pv_mm")
        rden_ready = sem("rden_ready")
        o_read = sem("o_read")
        g_sq = sem("g_sq")
        g_root = sem("g_root")
        g_rs = sem("g_rs")
        o_ready = sem("o_ready")
        ot_mm = sem("ot_mm")
        oh_ready = sem("oh_ready")
        o_split = sem("o_split")
        mem_loaded = sem("mem_loaded")
        memh_ready = sem("memh_ready")
        mem_ready = sem("mem_ready")
        vx_mm = sem("vx_mm")
        vx_out = sem("vx_out")
        s_msq = sem("s_msq")
        s_mmm = sem("s_mmm")
        s_mroot = sem("s_mroot")
        s_t5 = sem("s_t5")
        s_t5b = sem("s_t5b")
        scratch_out = sem("scratch_out")
        stored = sem("stored")
        passed = sem("passed")

        def wait_apart(e, sem_, value):
            e.wait_ge(sem_, value).then_inc(passed, 1)

        def wait_unit(e, L, u):
            e.wait_ge(unit_done, L * UNITS + u + 1 + USED0)

        def high(e, L, u, k, it=0):
            e.wait_ge(landed[u % 4], (L * (UNITS // 4) + (u // 4 + 1) + it) * 16)
            e.wait_ge(unit_done, L * UNITS + 4 * it + (u - 1 + USED0))
            e.activation(wh[u % 2][:, 0:k * P], raw[u % 4][:, 0:k * P], ACT.Copy).then_inc(high_ready, 1)

        def low(e, L, u, k, it=0):
            e.wait_ge(high_ready, L * UNITS + 4 * it + (u + 1))
            e.tensor_tensor(wl[u % 2][:, 0:k * P], raw[u % 4][:, 0:k * P],
                            wh[u % 2][:, 0:k * P].bitcast(F32), ALU.subtract).then_inc(split_ready, 1)

        block = ctx.enter_context(nc.Block())

        @block.sync
        def _(e):
            def load(L, u, src, k, it=0):
                e.wait_ge(split_ready, L * UNITS + 4 * it + (u - 3 + SPLIT0))
                e.dma_start(raw[u % 4][:, 0:k * P], src).then_inc(landed[u % 4], 16)

            for k in range(DT):
                e.dma_start(xT[:, k, :], x[k]).then_inc(x_loaded, 16)
            with e.Fori(0, LAYERS) as L:
                def ffn(f):
                    with e.Fori(0, FT // 2) as it:
                        for j in range(4):
                            load(L, U_IN[f] + j, w_first[bass.ds(L * 88 + it * 4 + (f * 44 + j), 1)].rearrange(
                                "a p n -> (a p) n"), DT, it)
                    with e.Fori(0, 4) as it:
                        for j in range(4):
                            load(L, U_OUT[f] + j, w_second[bass.ds(L * 32 + it * 4 + (f * 16 + j), 1)].rearrange(
                                "a p n -> (a p) n"), FH, it)

                ffn(0)
                with e.Fori(0, 16) as it:
                    for j in range(4):
                        load(L, U_HY + j, w_proj[bass.ds(L * 64 + it * 4 + j, 1)].rearrange(
                            "a p n -> (a p) n"), DT, it)
                ffn(1)
            for k in range(DT):
                e.wait_ge(x_ready, LAYERS * 32 - 7 + k + X0)
                e.dma_start(out[k], xT[:, k, :]).then_inc(stored, 16)
            e.wait_ge(stored, 16 * DT)

        @block.tensor
        def _(e):
            def unit(L, u, k, rH, rL, it=0, dest=None, first=True, last=True, n=T, k0=0):
                b = bank[u % 4 if dest is None else dest]
                e.wait_ge(split_ready, L * UNITS + 4 * it + (u + 1 + SPLIT0))
                if first:
                    e.wait_ge(evac, L * UNITS + 4 * it + (u - 3 + EVAC0))
                for kk in range(k):
                    cut = slice(kk * P, kk * P + P)
                    e.matmul(b[:, 0:n], wh[u % 2][:, cut], rH(k0 + kk), start=first and kk == 0, stop=False)
                    e.matmul(b[:, 0:n], wh[u % 2][:, cut], rL(k0 + kk), start=False, stop=False)
                    mm = e.matmul(b[:, 0:n], wl[u % 2][:, cut], rH(k0 + kk), start=False,
                                  stop=last and kk == k - 1)
                mm.then_inc(unit_done, 1)

            def u_of(k):
                return uH[:, k, :]

            def ul_of(k):
                return uL[:, k, :]

            def presums(L, a):
                for k in range(DT):
                    e.wait_ge(presq, L * 32 + (a * 8 + k + 1))
                    e.matmul(bank[6][:], ones[:], tmp[4 + k % 2][:], start=k == 0,
                             stop=k == DT - 1).then_inc(presum, 1)
                wait_apart(e, u_ready, L * 32 + (a * 8 + DT))

            def postsum_mm(L, a):
                e.wait_ge(postacc, L * 32 + (a * 8 + DT))
                e.matmul(bank[7][:], ones[:], tmp[0][:], start=True, stop=True).then_inc(postsum, 1)

            def ffn(L, f):
                presums(L, 3 * f)
                with e.Fori(0, FT // 2) as it:
                    for j in range(4):
                        unit(L, U_IN[f] + j, DT, u_of, ul_of, it)
                with e.Fori(0, 4) as it:
                    for j in range(4):
                        e.wait_ge(hid_split, L * 44 + (f * 22 + (FH if j == 0 else FT)))
                        unit(L, U_OUT[f] + j, FH, lambda k: hH[:, k * T:k * T + T], lambda k: hL[:, k * T:k * T + T],
                             it, dest=j // 2 * 2, first=j % 2 == 0, last=j % 2 == 1, k0=j % 2 * FH)
                postsum_mm(L, 3 * f)

            def attention(L, kind):
                first, n = {"A": (IT_A, 24), "C": (IT_C, 24), "X": (IT_X, 16)}[kind]
                g0 = {"A": GR_A, "C": GR_C, "X": GR_X}[kind]
                per = 2 if kind == "X" else 6
                chunks = 4 if kind == "C" else 2
                heads = 4 if kind == "X" else 6

                def ih(a):
                    return a // heads, a % heads

                for s in range(n + 6):
                    if s < n:
                        i, h = ih(s)
                        t = first + s
                        if s >= 2:
                            e.wait_ge(prob_ready, L * ITEMS + (t - 1))
                        S = bank[t % 2]
                        if kind == "X":
                            for c in range(2):
                                mm = e.matmul(S[:, 0:MEM], xa["qX"][:, 2 * h + c, i * P:i * P + P],
                                              xa["kX"][:, 2 * h + c, :], start=c == 0, stop=c == 1)
                        else:
                            lo, j = h % 2 * 64, h // 2
                            q, k = (at["qA"], at["kA"]) if kind == "A" else (at["qC"], at["kC"])
                            if kind == "A":
                                c0 = NA_START[i]
                                mm = e.matmul(S[:, 0:256], q[lo:lo + 64, j, i * P:i * P + P],
                                              k[lo:lo + 64, j, c0 * ROWS:c0 * ROWS + 256], start=True, stop=True)
                            else:
                                mm = e.matmul(S[:], q[lo:lo + 64, j, i * P:i * P + P], k[lo:lo + 64, j, :],
                                              start=True, stop=True)
                        mm.then_inc(score_mm, 1)
                    s2 = s - 2
                    if 0 <= s2 < n:
                        t = first + s2
                        e.wait_ge(prob_ready, L * ITEMS + (t + 1))
                        if s2 >= 2:
                            e.wait_ge(pt_ready, L * ITEMS + (t - 1))
                        for c in range(chunks):
                            mm = e.transpose(bank[2 + t % 2][:, c * P:c * P + P],
                                             tmp[t % 4][:, c * P:c * P + P], eye[:])
                        mm.then_inc(pt_mm, 1)
                    s3 = s - 3
                    if 0 <= s3 < n:
                        i, h = ih(s3)
                        t = first + s3
                        g = g0 + s3 // per
                        e.wait_ge(pt_ready, L * ITEMS + (t + 1))
                        if s3 % per == 0 and s3 // per >= 2:
                            e.wait_ge(o_read, L * GROUPS + (g - 1))
                        O = bank[4 + g % 2]
                        w = 256 if kind == "X" else 64
                        col = s3 % per * w
                        for c in range(chunks):
                            if kind == "X":
                                v = xa["VX"][:, c, h * 256:h * 256 + 256]
                            elif kind == "A":
                                v = at["VA"][:, NA_START[i] // 8 + 2 * c, h * 64:h * 64 + 64]
                            else:
                                v = at["VC"][:, c, h * 64:h * 64 + 64]
                            mm = e.matmul(O[:, col:col + w], tmp[4 + t % 2][:, c * P:c * P + P], v,
                                          start=c == 0, stop=c == chunks - 1)
                        mm.then_inc(pv_mm, 1)
                    s5 = s - 5
                    if 0 <= s5 < n and s5 % per == per - 1:
                        g = g0 + s5 // per
                        e.wait_ge(o_ready, L * GROUPS + (g + 1))
                        if s5 // per >= 2:
                            e.wait_ge(o_split, L * 32 + o_count(kind, s5 // per - 2) + oh_per(kind))
                        w = 4 if kind == "X" else 3
                        for c in range(w):
                            mm = e.transpose(bank[6 + g % 2][:, c * P:c * P + P], on[:, c * P:c * P + P], eye[:])
                        mm.then_inc(ot_mm, 1)

            for k in range(DT):
                e.wait_ge(const_set, 1)
                e.wait_ge(s_msq, k + 1)
                e.matmul(bank[6][:, 0:MEM], ones[:], tmp[4 + k % 2][:, 0:MEM], start=k == 0,
                         stop=k == DT - 1).then_inc(s_mmm, 1)
            e.wait_ge(setup_loaded, 16 * 5)
            for c in range(2):
                e.matmul(bank[c][0:C_H, :], st["t5s"][0:32, 0:C_H], st["hot"][0:32, c * T:c * T + T],
                         start=True, stop=True).then_inc(s_t5, 1)
            e.wait_ge(s_t5b, 2)
            e.sem_inc(unit_done, USED0)

            with e.Fori(0, LAYERS) as L:
                ffn(L, 0)

                presums(L, 1)
                for j in range(6):
                    unit(L, U_HY + j, DT, u_of, ul_of)
                    if j == 0:
                        wait_apart(e, hy_loaded, L * 176 + 176)
                        e.matmul(bank[4][0:FW, :], hy["w1"][0:EMB, :], hy["emb"][0:EMB, :], start=True,
                                 stop=True).then_inc(f_mm, 1)
                    elif j <= 2:
                        wait_apart(e, f_sin, L * 3 + j)
                        e.matmul(bank[4][0:FW, :], hy[f"w{j + 1}"][0:FW, :], tmp[3][0:FW, :], start=True,
                                 stop=True).then_inc(f_mm, 1)
                    elif j == 3:
                        e.wait_ge(f_sin, L * 3 + 3)
                        for m in range(4):
                            e.matmul(bank[4 + m][:], tmp[3][0:FW, m * P:m * P + P], hy["w4"][0:FW, :],
                                     start=True, stop=True).then_inc(taps_mm, 1)
                    elif j == 5:
                        e.wait_ge(taps_ready, L * 7 + 7)
                        for part in range(2):
                            for half in range(2):
                                for kt in (2 * half, 2 * half + 1):
                                    for m in range(4):
                                        rhs = hy["even"][:, m, :] if part == 0 else hy["taps"][:, m, 256:512]
                                        mm = e.matmul(bank[4 + 2 * part + half][:, kt % 2 * 256:kt % 2 * 256 + 256],
                                                      hy["fwd"][:, part, m, kt * P:kt * P + P], rhs,
                                                      start=m == 0, stop=m == 3)
                                mm.then_inc(filt_mm, 1)
                for half in range(2):
                    e.wait_ge(z_ready, L * 2 + 2)
                    e.wait_ge(filt_ready, L * 4 + 4)
                    for tt in (2 * half, 2 * half + 1):
                        for c in range(HYT):
                            mm = e.transpose(bank[4 + half][:, (tt % 2 * 2 + c) * P:(tt % 2 * 2 + c) * P + P],
                                             hy["uc"][:, c, tt * P:tt * P + P], eye[:])
                    mm.then_inc(zt_mm, 1)
                e.wait_ge(zt_ready, L * 2 + 2)
                for part in range(2):
                    for half in range(2):
                        for kt in (2 * half, 2 * half + 1):
                            for m in range(4):
                                mm = e.matmul(bank[6 - 2 * part + half][:, kt % 2 * 256:kt % 2 * 256 + 256],
                                              hy["fwd"][:, part, m, kt * P:kt * P + P], hy["zt"][:, m, :],
                                              start=m == 0, stop=m == 3)
                        mm.then_inc(z_mm, 1)
                e.wait_ge(prod, L * 12 + 12)
                for c in range(HYT):
                    for part in range(2):
                        for kt in range(4):
                            mm = e.matmul(bank[4 + c][:], hy["taps"][:, kt, part * 256 + c * P:part * 256 + c * P + P],
                                          hy["inv"][:, part, kt, :], start=part + kt == 0, stop=part == 1 and kt == 3)
                    mm.then_inc(y_mm, 1)
                for c in range(HYT):
                    e.wait_ge(hysq, L * 2 + c + 1)
                    mm = e.matmul(bank[6][:], ones[:], tmp[4 + c][:], start=c == 0, stop=c == 1)
                mm.then_inc(hysum, 1)

                def turn_values(j):
                    e.wait_ge(evac, L * UNITS + (U_VA + j + 1 + EVAC0))
                    vt = at["vt"][:, j % 3, :]
                    if j < 3:
                        for half in range(2):
                            if j >= 1:
                                e.wait_ge(vt_out, L * 9 + 2 * j - 1 + half)
                            for n, c in enumerate(NA_CHUNKS[4 * half:4 * half + 4]):
                                mm = e.transpose(bank[4 + half][:, n * P:n * P + P], vt[:, c * ROWS:c * ROWS + P], eye[:])
                            mm.then_inc(vt_mm, 1)
                    else:
                        b = (4, 5, 4)[j - 3]
                        e.wait_ge(vt_out, L * 9 + (5, 6, 7)[j - 3])
                        for n in range(4):
                            mm = e.transpose(bank[b][:, n * P:n * P + P], vt[:, n * P:n * P + P], eye[:])
                        mm.then_inc(vt_mm, 1)

                for j in range(18):
                    unit(L, U_VA + j, DT, u_of, ul_of)
                    if 1 <= j <= 6:
                        turn_values(j - 1)
                e.wait_ge(evac, L * UNITS + (U_WO + EVAC0))
                e.wait_ge(vt_out, L * 9 + 9)
                e.wait_ge(m_ready, L * 2 + 2)
                attention(L, "A")
                attention(L, "C")
                e.wait_ge(o_split, L * 32 + 24)
                for j in range(8):
                    unit(L, U_WO + j, DT, u_of, ul_of)
                postsum_mm(L, 1)

                presums(L, 2)
                for j in range(8):
                    unit(L, U_XQ + j, DT, u_of, ul_of)
                e.wait_ge(mem_ready, L * 8 + 8)
                for j in range(16):
                    unit(L, U_XK + j, DT, lambda k: xa["memH"][:, k, :], lambda k: xa["memL"][:, k, :], n=MEM)
                for j in range(8):
                    e.wait_ge(evac, L * UNITS + (U_XV + j + 1 + EVAC0))
                    if j >= 2:
                        e.wait_ge(vx_out, L * 8 + j - 1)
                    for m in range(2):
                        mm = e.transpose(bank[4 + j % 2][:, m * P:m * P + P], xa["vX"][:, j, m * P:m * P + P], eye[:])
                    mm.then_inc(vx_mm, 1)
                e.wait_ge(vx_out, L * 8 + 8)
                attention(L, "X")
                e.wait_ge(o_split, L * 32 + 32)
                for j in range(8):
                    unit(L, U_XO + j, DT, u_of, ul_of)
                postsum_mm(L, 2)
                ffn(L, 1)

        @block.scalar
        def _(e):
            def prenorm(L, a, k):
                e.wait_ge(x_ready, L * 32 + ((a * 8 - 7 + k if a else 0) + X0))
                e.activation(uH[:, k, :], xT[:, k, :], ACT.Copy,
                             scale=pr[:, G0 + PRE[a] * 8 + k:G0 + PRE[a] * 8 + k + 1]).then_inc(uh_ready, 1)
                if k >= 2:
                    e.wait_ge(presum, L * 32 + (a * 8 + k - 1))
                e.activation(tmp[4 + k % 2][:], xT[:, k, :], ACT.Square).then_inc(presq, 1)

            def preroot_(L, a):
                e.wait_ge(presum, L * 32 + (a * 8 + DT))
                e.activation(rs[:], bank[6][:], ACT.Sqrt, scale=1.0 / D, bias=epsc[:, 0:1]).then_inc(preroot, 1)

            def postroot_(L, a):
                half = a in (0, 3)
                e.wait_ge(postsum, L * 4 + (a + 1))
                e.activation(rsp[:], bank[7][:], ACT.Sqrt, scale=(4.0 if half else 1.0) / D,
                             bias=epsc[:, 1:2] if half else epsc[:, 0:1]).then_inc(postroot, 1)

            def y_tile(L, a, j, src, dst, inc, it=None):
                k = j if it is None else 2 * it + j
                if it is None and j >= 2:
                    e.wait_ge(postacc, L * 32 + (a * 8 + j - 1))
                e.activation(tmp[4 + j % 2][:], src[:], ACT.Square).then_inc(postsq, 1)
                e.activation(dst, src[:], ACT.Copy).then_inc(evac, inc)

            def ffn(L, f):
                a = 3 * f
                if f == 0:
                    e.wait_ge(params_loaded, L * 16 + 16)
                    for k in range(DT):
                        prenorm(L, 0, k)
                    high(e, L, U_IN[0], DT)
                    high(e, L, U_IN[0] + 1, DT)
                preroot_(L, a)
                def pair(q, it, ahead):
                    p = L * 44 + 2 * it + (f * 22 + q)
                    if ahead:
                        high(e, L, U_IN[f] + 2 * q + 2, DT, it)
                    e.wait_ge(gate_scaled, p + 1)
                    e.activation(tmp[q][:], tmp[q][:], ACT.Silu).then_inc(silu_ready, 1)
                    if ahead:
                        high(e, L, U_IN[f] + 2 * q + 3, DT, it)
                    e.wait_ge(hid_ready, p + 1)
                    e.activation(hH[:, bass.ds((2 * it + q) * T, T)], tmp[2 + q][:], ACT.Copy).then_inc(hidh_ready, 1)
                with e.Fori(0, FT // 2 - 1) as it:
                    pair(0, it, True)
                    pair(1, it, True)
                last = FT // 2 - 1
                pair(0, last, True)
                high(e, L, U_OUT[f], FH)
                pair(1, last, False)
                high(e, L, U_OUT[f] + 1, FH)

                def tile(q, it, ahead):
                    u = U_OUT[f] + 2 * q
                    if ahead:
                        high(e, L, u + 2, FH, it)
                        high(e, L, u + 3, FH, it)
                    else:
                        e.wait_ge(unit_done, L * UNITS + 4 * it + (u + 2 + USED0))
                    e.wait_ge(postacc, L * 32 + 2 * it + (a * 8 + q - 1)) if not (isinstance(it, int) and it == 0) else None
                    e.activation(tmp[4 + q][:], bank[2 * q][:], ACT.Square).then_inc(postsq, 1)
                    e.activation(yf[:, bass.ds(2 * it + q, 1), :].rearrange("p a n -> p (a n)"), bank[2 * q][:],
                                 ACT.Copy).then_inc(evac, 2)
                tile(0, 0, True)
                tile(1, 0, True)
                with e.Fori(1, 3) as it:
                    tile(0, it, True)
                    tile(1, it, True)
                tile(0, 3, True)
                tile(1, 3, False)
                postroot_(L, a)

            def attention(L, kind):
                first, n = {"A": (IT_A, 24), "C": (IT_C, 24), "X": (IT_X, 16)}[kind]
                g0 = {"A": GR_A, "C": GR_C, "X": GR_X}[kind]
                per = 2 if kind == "X" else 6
                wide = 512 if kind == "C" else 256
                for s in range(n + 6):
                    if s < n:
                        t = first + s
                        e.wait_ge(biased, L * ITEMS + (t + 1))
                        if kind == "X" and s >= 4:
                            e.wait_ge(pt_mm, L * ITEMS + (t - 3))
                        src = bank[t % 2][:, 0:wide] if kind == "X" else tmp[t % 4][:, 0:wide]
                        e.activation(tmp[t % 4][:, 0:wide], src, ACT.Exp, scale=-1.0, bias=negmax[:, t:t + 1],
                                     accum_out=den[:, t:t + 1]).then_inc(prob_ready, 1)
                    s2 = s - 2
                    if 0 <= s2 < n:
                        t = first + s2
                        e.wait_ge(pt_mm, L * ITEMS + (t + 1))
                        if s2 >= 2:
                            e.wait_ge(pv_mm, L * ITEMS + (t - 1))
                        e.activation(tmp[4 + t % 2][:, 0:wide], bank[2 + t % 2][:, 0:wide],
                                     ACT.Copy).then_inc(pt_ready, 1)
                    s3 = s - 3
                    if kind != "X" and 0 <= s3 < n and s3 % per == per - 1:
                        g = g0 + s3 // per
                        e.wait_ge(g_sq, L * 8 + (g + 1))
                        e.activation(gss[:, 1, g:g + 1], gss[:, 0, g:g + 1], ACT.Sqrt, scale=1.0 / 384,
                                     bias=epsc[:, 0:1]).then_inc(g_root, 1)
                    s5 = s - 5
                    if 0 <= s5 < n and s5 % per == per - 1:
                        g = g0 + s5 // per
                        e.wait_ge(ot_mm, L * GROUPS + (g + 1))
                        if kind == "X":
                            dst, src = x_out(uH, g - GR_X), bank[6 + g % 2][:].rearrange("p (c n) -> p c n", c=4)
                            e.activation(dst, src, ACT.Copy).then_inc(oh_ready, 1)
                        else:
                            for c in range(3):
                                dst, src, k = ac_out(uH, kind, g % 4, c)
                                e.activation(dst, src(bank[6 + g % 2]), ACT.Copy,
                                             scale=pr[:, G0 + G_GROUP * 8 + k:G0 + G_GROUP * 8 + k + 1]
                                             ).then_inc(oh_ready, 1)

            e.wait_ge(setup_loaded, 16 * 5)
            for k in range(DT):
                if k >= 2:
                    e.wait_ge(s_mmm, k - 1)
                e.activation(tmp[4 + k % 2][:, 0:MEM], st["memS"][:, k, :], ACT.Square).then_inc(s_msq, 1)
            e.wait_ge(s_mmm, DT)
            e.wait_ge(const_set, 1)
            e.activation(rsm[:], bank[6][:, 0:MEM], ACT.Sqrt, scale=1.0 / D, bias=epsc[:, 0:1]).then_inc(s_mroot, 1)

            with e.Fori(0, LAYERS) as L:
                ffn(L, 0)
                high(e, L, U_HY, DT)
                high(e, L, U_HY + 1, DT)
                for k in range(DT):
                    prenorm(L, 1, k)
                preroot_(L, 1)
                for j in range(6):
                    high(e, L, U_HY + j + 2, DT)
                    if j < 3:
                        e.wait_ge(f_bias, L + 1)
                        e.wait_ge(f_mm, L * 3 + j + 1)
                        e.activation(tmp[1][0:FW, :], bank[4][0:FW, :], ACT.Identity, scale=hy["fv"][0:FW, 3:4],
                                     bias=hy["fv"][0:FW, 4 + j:5 + j]).then_inc(f_arg, 1)
                        e.wait_ge(f_red, L * 15 + 5 * j + 5)
                        e.activation(tmp[3][0:FW, :], tmp[1][0:FW, :], ACT.Sin).then_inc(f_sin, 1)
                    if j == 3:
                        e.wait_ge(hy_loaded, L * 176 + 176)
                        e.activation(tmp[0][:], tmp[0][:], ACT.Abs).then_inc(absd, 1)
                        e.wait_ge(absd, L + 1)
                        for m in range(4):
                            if m >= 2:
                                e.wait_ge(taps_ready, L * 7 + m - 1)
                            e.activation(tmp[1 + m % 2][:], tmp[0][:], ACT.Exp,
                                         scale=hy["tneg"][:, m:m + 1]).then_inc(window, 1)
                for n in range(4):
                    e.wait_ge(filt_mm, L * 4 + n + 1)
                    e.activation(hy["filt"][:, n // 2, n % 2 * 2:n % 2 * 2 + 2, :],
                                 bank[4 + n][:].rearrange("p (k c) -> p k c", k=2), ACT.Copy).then_inc(filt_ready, 1)
                for n in range(2):
                    e.wait_ge(zt_mm, L * 2 + n + 1)
                    e.activation(hy["zt"][:, 2 * n:2 * n + 2, :], bank[4 + n][:].rearrange("p (k c) -> p k c", k=2),
                                 ACT.Copy).then_inc(zt_ready, 1)
                for c in range(HYT):
                    e.wait_ge(hyout, L * 7 + 2 * c + 2)
                    e.activation(tmp[4 + c][:], yb[c][:], ACT.Square).then_inc(hysq, 1)
                e.wait_ge(hysum, L + 1)
                e.activation(rsp[:], bank[6][:], ACT.Sqrt, scale=1.0 / (HYT * P), bias=epsc[:, 0:1]).then_inc(hyroot, 1)
                for j in range(18):
                    if j < 16:
                        high(e, L, U_VA + j + 2, DT)
                    if 1 <= j <= 3:
                        for half in range(2):
                            e.wait_ge(vt_mm, L * 9 + 2 * (j - 1) + half + 1)
                            w = 4 - half
                            e.activation(at["VA"][:, 4 * half:4 * half + w, (j - 1) * P:j * P],
                                         bank[4 + half][:, 0:w * P].rearrange("p (n c) -> p n c", n=w),
                                         ACT.Copy).then_inc(vt_out, 1)
                    elif 4 <= j <= 6:
                        e.wait_ge(vt_mm, L * 9 + j + 3)
                        e.activation(at["VC"][:, :, (j - 4) * P:(j - 3) * P],
                                     bank[(4, 5, 4)[j - 4]][:].rearrange("p (n c) -> p n c", n=4),
                                     ACT.Copy).then_inc(vt_out, 1)
                e.wait_ge(unit_done, L * UNITS + (U_WO + USED0))
                e.wait_ge(hyout, L * 7 + 7)
                for c in range(HYT):
                    e.activation(uH[:, 3 + c, :], yb[c][:], ACT.Copy).then_inc(ybh, 1)
                high(e, L, U_WO, DT)
                high(e, L, U_WO + 1, DT)
                attention(L, "A")
                attention(L, "C")
                def out_tiles(base, a):
                    for j in range(8):
                        if j < 6:
                            high(e, L, base + j + 2, DT)
                        else:
                            wait_unit(e, L, base + j)
                        y_tile(L, a, j, bank[(base + j) % 4], xa["yx"][:, j, :], 1)
                    postroot_(L, a)
                out_tiles(U_WO, 1)
                high(e, L, U_XQ, DT)
                high(e, L, U_XQ + 1, DT)
                for k in range(DT):
                    prenorm(L, 2, k)
                preroot_(L, 2)
                for j in range(24):
                    if j < 22:
                        high(e, L, U_XQ + j + 2, DT)
                    if j == 0:
                        e.wait_ge(mem_loaded, L * 16 + 16)
                    if j < 8:
                        e.activation(xa["memH"][:, j, :], xa["memT"][:, j, :], ACT.Copy,
                                     scale=pr[:, G0 + G_MEM * 8 + j:G0 + G_MEM * 8 + j + 1]).then_inc(memh_ready, 1)
                for j in range(8):
                    e.wait_ge(vx_mm, L * 8 + j + 1)
                    e.activation(xa["VX"][:, :, j * P:j * P + P],
                                 bank[4 + j % 2][:, 0:MEM].rearrange("p (m c) -> p m c", m=2),
                                 ACT.Copy).then_inc(vx_out, 1)
                high(e, L, U_XO, DT)
                high(e, L, U_XO + 1, DT)
                attention(L, "X")
                out_tiles(U_XO, 2)
                high(e, L, U_IN[1], DT)
                high(e, L, U_IN[1] + 1, DT)
                for k in range(DT):
                    prenorm(L, 3, k)
                ffn(L, 1)

        @block.vector
        def _(e):
            def update(L, a, k, y):
                t = tmp[1 + k % 2]
                e.scalar_tensor_tensor(t[:], y[:, k, :], pr[:, G0 + POST[a] * 8 + k:G0 + POST[a] * 8 + k + 1],
                                       rsp[:], ALU.mult, ALU.mult).then_inc(y_scaled, 1)
                e.wait_ge(y_scaled, L * 32 + (a * 8 + k + 1))
                e.tensor_tensor(xT[:, k, :], xT[:, k, :], t[:], ALU.add).then_inc(x_ready, 1)

            def low_u(L, a, k):
                e.wait_ge(uh_ready, L * 32 + (a * 8 + k + 1))
                e.scalar_tensor_tensor(uL[:, k, :], xT[:, k, :], pr[:, G0 + PRE[a] * 8 + k:G0 + PRE[a] * 8 + k + 1],
                                       uH[:, k, :].bitcast(F32), ALU.mult, ALU.subtract).then_inc(u_ready, 1)

            def post_rs(L, a):
                e.wait_ge(postroot, L * 4 + (a + 1))
                e.reciprocal(rsp[:], rsp[:]).then_inc(rsp_ready, 1)
                e.wait_ge(rsp_ready, L * 4 + (a + 1))

            def pre_rs(L, a):
                e.wait_ge(preroot, L * 4 + (a + 1))
                e.reciprocal(rs[:], rs[:]).then_inc(rs_ready, 1)
                wait_apart(e, rs_ready, L * 4 + (a + 1))

            def boundary(L, a, y):
                post_rs(L, a)
                for k in range(DT + 1):
                    if k < DT:
                        update(L, a, k, y)
                    if k >= 1:
                        e.wait_ge(x_ready, L * 32 + (a * 8 + k + X0))
                        low_u(L, a + 1, k - 1)
                pre_rs(L, a + 1)

            def add_square(L, a, j, it=0):
                n = L * 32 + 2 * it + (a * 8 + j)
                e.wait_ge(postsq, n + 1)
                if j == 0 and isinstance(it, int) and it == 0:
                    e.tensor_copy(tmp[0][:], tmp[4][:]).then_inc(postacc, 1)
                else:
                    e.wait_ge(postacc, n)
                    e.tensor_tensor(tmp[0][:], tmp[0][:], tmp[4 + j % 2][:], ALU.add).then_inc(postacc, 1)

            def ffn(L, f):
                a = 3 * f
                if f == 0:
                    e.wait_ge(params_loaded, L * 16 + 16)
                    e.wait_ge(x_ready, L * 32 + X0)
                    for k in range(DT):
                        low_u(L, 0, k)
                    low(e, L, U_IN[0], DT)
                    low(e, L, U_IN[0] + 1, DT)
                    pre_rs(L, 0)

                def pair(q, it, ahead):
                    p = L * 44 + 2 * it + (f * 22 + q)
                    u = U_IN[f] + 2 * q
                    n = L * UNITS + 4 * it
                    e.wait_ge(unit_done, n + (u + 1 + USED0))
                    e.tensor_tensor(tmp[q][:], bank[u % 4][:], rs[:], ALU.mult).then_inc(gate_scaled, 1)
                    if ahead:
                        low(e, L, u + 2, DT, it)
                    e.wait_ge(unit_done, n + (u + 2 + USED0))
                    e.tensor_tensor(tmp[2 + q][:], bank[u % 4 + 1][:], rs[:], ALU.mult).then_inc(evac, 2)
                    if ahead:
                        low(e, L, u + 3, DT, it)
                    e.wait_ge(evac, n + (u + 2 + EVAC0))
                    e.wait_ge(silu_ready, p + 1)
                    e.tensor_tensor(tmp[2 + q][:], tmp[q][:], tmp[2 + q][:], ALU.mult).then_inc(hid_ready, 1)
                    e.wait_ge(hidh_ready, p + 1)
                    at_ = bass.ds((2 * it + q) * T, T)
                    e.tensor_tensor(hL[:, at_], tmp[2 + q][:], hH[:, at_].bitcast(F32),
                                    ALU.subtract).then_inc(hid_split, 1)
                with e.Fori(0, FT // 2 - 1) as it:
                    pair(0, it, True)
                    pair(1, it, True)
                last = FT // 2 - 1
                pair(0, last, True)
                low(e, L, U_OUT[f], FH)
                pair(1, last, False)
                low(e, L, U_OUT[f] + 1, FH)

                def tile(q, it, ahead):
                    u = U_OUT[f] + 2 * q
                    if ahead:
                        low(e, L, u + 2, FH, it)
                        low(e, L, u + 3, FH, it)
                    add_square(L, a, q, it)
                tile(0, 0, True)
                tile(1, 0, True)
                with e.Fori(1, 3) as it:
                    tile(0, it, True)
                    tile(1, it, True)
                tile(0, 3, True)
                tile(1, 3, False)

            def attention(L, kind):
                first, n = {"A": (IT_A, 24), "C": (IT_C, 24), "X": (IT_X, 16)}[kind]
                g0 = {"A": GR_A, "C": GR_C, "X": GR_X}[kind]
                per = 2 if kind == "X" else 6
                heads = 4 if kind == "X" else 6
                w = 256 if kind == "X" else 64
                for s in range(n + 6):
                    if s < n:
                        i, h = s // heads, s % heads
                        t = first + s
                        wait_apart(e, score_mm, L * ITEMS + (t + 1))
                        S = bank[t % 2]
                        if kind == "X":
                            e.tensor_reduce(negmax[:, t:t + 1], S[:, 0:MEM], AX.X, ALU.min).then_inc(biased, 1)
                        else:
                            if s >= 4:
                                wait_apart(e, pt_mm, L * ITEMS + (t - 3))
                            if kind == "A":
                                width, bias = 256, at["biasA"][:, (0, 1, 1, 2)[i], h, :]
                            else:
                                width, bias = 512, strip[:, h, (3 - i) * P:(3 - i) * P + T]
                            e.tensor_tensor_reduce(tmp[t % 4][:, 0:width], S[:, 0:width], bias, 1.0, 3.0e38,
                                                   ALU.add, ALU.min, negmax[:, t:t + 1]).then_inc(biased, 1)
                    s3 = s - 3
                    if 0 <= s3 < n and s3 % per == per - 1:
                        g = g0 + s3 // per
                        t = first + s3
                        lo = t - per + 1
                        e.wait_ge(prob_ready, L * ITEMS + (t + 1))
                        e.reciprocal(rden[:, lo:t + 1], den[:, lo:t + 1]).then_inc(rden_ready, 1)
                        e.wait_ge(rden_ready, L * GROUPS + (g + 1))
                        e.wait_ge(pv_mm, L * ITEMS + (t + 1))
                        if s3 // per >= 1:
                            e.wait_ge(ot_mm, L * GROUPS + g)
                        last = e.tensor_tensor(
                            on[:, 0:per * w].rearrange("p (h c) -> p h c", h=per),
                            bank[4 + g % 2][:, 0:per * w].rearrange("p (h c) -> p h c", h=per),
                            rden[:, lo:t + 1].unsqueeze(2).to_broadcast([P, per, w]), ALU.mult)
                        last.then_inc(o_read, 1)
                        e.wait_ge(o_read, L * GROUPS + (g + 1))
                        if kind != "X":
                            e.tensor_tensor_reduce(yx_free(L)[:, 0:384], on[:, 0:384], on[:, 0:384], 1.0, 0.0,
                                                   ALU.mult, ALU.add, gss[:, 0, g:g + 1]).then_inc(g_sq, 1)
                            e.wait_ge(g_root, L * 8 + (g + 1))
                            e.reciprocal(gss[:, 2, g:g + 1], gss[:, 1, g:g + 1]).then_inc(g_rs, 1)
                            e.wait_ge(g_rs, L * 8 + (g + 1))
                            e.tensor_scalar(on[:, 0:384], on[:, 0:384], gss[:, 2, g:g + 1], None,
                                            ALU.mult).then_inc(o_ready, 1)
                        else:
                            e.sem_inc(o_ready, 1)
                    s5 = s - 5
                    if 0 <= s5 < n and s5 % per == per - 1:
                        g = g0 + s5 // per
                        b = bank[6 + g % 2]
                        if kind == "X":
                            e.wait_ge(oh_ready, L * 32 + (24 + g - GR_X + 1))
                            e.tensor_tensor(x_out(uL, g - GR_X), b[:].rearrange("p (c n) -> p c n", c=4),
                                            x_out(uH, g - GR_X).bitcast(F32), ALU.subtract).then_inc(o_split, 1)
                        else:
                            e.wait_ge(oh_ready, L * 32 + (3 * g + 3))
                            for c in range(3):
                                dst, src, k = ac_out(uL, kind, g % 4, c)
                                hi = ac_out(uH, kind, g % 4, c)[0].bitcast(F32)
                                e.scalar_tensor_tensor(dst, src(b),
                                                       pr[:, G0 + G_GROUP * 8 + k:G0 + G_GROUP * 8 + k + 1],
                                                       hi, ALU.mult, ALU.subtract).then_inc(o_split, 1)

            def yx_free(L):
                return rsq

            e.memset(ones[:], 1.0)
            e.memset(epsc[:, 0:1], EPS)
            e.memset(epsc[:, 1:2], 4 * EPS).then_inc(const_set, 1)
            e.sem_inc(split_ready, SPLIT0)
            e.sem_inc(evac, EVAC0)
            e.wait_ge(setup_loaded, 16 * 5)
            for c in range(2):
                e.wait_ge(s_t5, c + 1)
                e.tensor_tensor(st["lnn"][0:C_H, c * T:c * T + T], st["lnn"][0:C_H, c * T:c * T + T],
                                bank[c][0:C_H, :], ALU.subtract).then_inc(s_t5b, 1)
            e.wait_ge(s_mroot, 1)
            e.reciprocal(rsm[:], rsm[:])
            e.wait_ge(x_loaded, 16 * DT)
            e.sem_inc(x_ready, X0)

            with e.Fori(0, LAYERS) as L:
                ffn(L, 0)
                low(e, L, U_HY, DT)
                low(e, L, U_HY + 1, DT)
                boundary(L, 0, yf)
                e.memset(hy["p"][:, :, 0:1], 0.0)
                e.memset(hy["p"][:, :, T + 1:T + 2], 0.0).then_inc(pad_zero, 1)
                e.wait_ge(pad_zero, L + 1)
                fv = hy["fv"]
                e.wait_ge(hy_loaded, L * 176 + 176)
                e.tensor_scalar(fv[0:FW, 4:7], fv[0:FW, 0:3], fv[0:FW, 3:4], None, ALU.mult).then_inc(f_bias, 1)
                for j in range(6):
                    low(e, L, U_HY + j + 2, DT)
                    wait_unit(e, L, U_HY + j)
                    p = hy["p"]
                    c = hy["uc"][:, j, :]
                    cw = [pr[:, CW0 + 6 * n + j:CW0 + 6 * n + j + 1] for n in range(3)]
                    e.tensor_tensor(p[:, j, 1:T + 1], bank[(U_HY + j) % 4][:], rs[:], ALU.mult).then_inc(evac, 1)
                    e.wait_ge(evac, L * UNITS + (U_HY + j + 1 + EVAC0))
                    e.tensor_scalar(c, p[:, j, 0:T], cw[0], pr[:, CB0 + j:CB0 + j + 1], ALU.mult,
                                    ALU.add).then_inc(conv, 1)
                    for n in (1, 2):
                        e.wait_ge(conv, L * 18 + (3 * j + n))
                        e.scalar_tensor_tensor(c, p[:, j, n:n + T], cw[n], c, ALU.mult, ALU.add).then_inc(conv, 1)
                    if j < 3:
                        a, n = tmp[1][0:FW, :], tmp[2][0:FW, :]
                        r = L * 15 + 5 * j
                        e.wait_ge(f_arg, L * 3 + j + 1)
                        e.tensor_scalar(n, a, 1 / (2 * math.pi), ROUND, ALU.mult, ALU.add).then_inc(f_red, 1)
                        e.wait_ge(f_red, r + 1)
                        e.tensor_scalar(n, n, ROUND, None, ALU.subtract).then_inc(f_red, 1)
                        e.wait_ge(f_red, r + 2)
                        e.scalar_tensor_tensor(a, n, -TWO_PI_HI, a, ALU.mult, ALU.add).then_inc(f_red, 1)
                        e.wait_ge(f_red, r + 3)
                        e.scalar_tensor_tensor(a, n, -TWO_PI_LO, a, ALU.mult, ALU.add).then_inc(f_red, 1)
                        e.wait_ge(f_red, r + 4)
                        e.tensor_scalar(a, a, -PI_IN, PI_IN, ALU.max, ALU.min).then_inc(f_red, 1)
                    if j == 3:
                        for m in range(4):
                            e.wait_ge(window, L * 4 + m + 1)
                            e.wait_ge(taps_mm, L * 4 + m + 1)
                            e.tensor_tensor(hy["taps"][:, m, :], bank[4 + m][:], tmp[1 + m % 2][:],
                                            ALU.mult).then_inc(taps_ready, 1)
                        e.wait_ge(taps_ready, L * 7 + 4)
                        e.memset(hy["taps"][0:1, 0, 256:512], 0.0).then_inc(taps_ready, 1)
                        e.wait_ge(taps_ready, L * 7 + 5)
                        e.tensor_tensor(hy["even"][:], hy["taps"][:, :, 0:256], hy["taps"][:, :, 256:512],
                                        ALU.add).then_inc(taps_ready, 1)
                        e.tensor_tensor(hy["taps"][:, :, 256:512], hy["taps"][:, :, 256:512],
                                        hy["taps"][:, :, 0:256], ALU.subtract).then_inc(taps_ready, 1)
                e.wait_ge(conv, L * 18 + 12)
                for c in range(HYT):
                    e.tensor_tensor(hy["uc"][:, c, :], hy["uc"][:, 2 + c, :], hy["uc"][:, c, :],
                                    ALU.mult).then_inc(z_ready, 1)
                e.wait_ge(filt_ready, L * 4 + 4)
                e.wait_ge(z_mm, L * 4 + 4)
                for half in range(2):
                    ks = slice(2 * half, 2 * half + 2)
                    zc = bank[6 + half][:].rearrange("p (k c) -> p k c", k=2)
                    zs = bank[4 + half][:].rearrange("p (k c) -> p k c", k=2)
                    fe, fo = hy["filt"][:, 0, ks, :], hy["filt"][:, 1, ks, :]
                    yr, yn, t = hy["taps"][:, ks, 0:256], hy["taps"][:, ks, 256:512], hy["even"][:, ks, :]
                    r = L * 12 + 6 * half
                    e.tensor_tensor(yr, zc, fe, ALU.mult).then_inc(prod, 1)
                    e.tensor_tensor(t, zs, fo, ALU.mult).then_inc(prod, 1)
                    e.wait_ge(prod, r + 2)
                    e.tensor_tensor(yr, yr, t, ALU.add).then_inc(prod, 1)
                    e.tensor_tensor(yn, zs, fe, ALU.mult).then_inc(prod, 1)
                    e.wait_ge(prod, r + 3)
                    e.tensor_tensor(t, zc, fo, ALU.mult).then_inc(prod, 1)
                    e.wait_ge(prod, r + 5)
                    e.tensor_tensor(yn, yn, t, ALU.subtract).then_inc(prod, 1)
                for c in range(HYT):
                    e.wait_ge(y_mm, L * 2 + c + 1)
                    e.wait_ge(z_ready, L * 2 + 2)
                    e.scalar_tensor_tensor(yb[c][:], hy["uc"][:, c, :], pr[:, SK0 + c:SK0 + c + 1],
                                           bank[4 + c][:], ALU.mult, ALU.add).then_inc(hyout, 1)
                    e.wait_ge(conv, L * 18 + 18)
                    e.wait_ge(hyout, L * 7 + 2 * c + 1)
                    e.tensor_tensor(yb[c][:], yb[c][:], hy["uc"][:, 4 + c, :], ALU.mult).then_inc(hyout, 1)
                e.wait_ge(hyroot, L + 1)
                e.reciprocal(rsp[:], rsp[:]).then_inc(hyout, 1)
                e.wait_ge(hyout, L * 7 + 5)
                for c in range(HYT):
                    e.scalar_tensor_tensor(yb[c][:], yb[c][:], pr[:, G0 + G_GROUP * 8 + 3 + c:G0 + G_GROUP * 8 + 4 + c],
                                           rsp[:], ALU.mult, ALU.mult).then_inc(hyout, 1)
                e.tensor_scalar(rsq[:], rs[:], -0.125, None, ALU.mult).then_inc(rsq_ready, 1)
                e.wait_ge(rsq_ready, L + 1)
                for j in range(18):
                    if j < 16:
                        low(e, L, U_VA + j + 2, DT)
                    wait_unit(e, L, U_VA + j)
                    b = bank[(U_VA + j) % 4]
                    if j < 6:
                        if j >= 3:
                            e.wait_ge(vt_mm, L * 9 + 2 * (j - 3) + 2)
                        dst = at["vt"][:, j % 3, :]
                        if j < 3:
                            e.tensor_tensor(by_column(dst), by_row(b[:]), by_row(rs[:]), ALU.mult).then_inc(evac, 1)
                        else:
                            e.tensor_tensor(dst, b[:], rs[:], ALU.mult).then_inc(evac, 1)
                    elif j < 9:
                        def grid(ap):
                            return ap.rearrange("p (r i c) -> p i r c", r=ROWS, i=4)
                        back = at["qA"][:, j - 6, ::-1].rearrange("p (i r c) -> p i r c", i=4, r=ROWS)[:, ::-1]
                        e.tensor_tensor(back, grid(b[:]), grid(rsq[:]), ALU.mult).then_inc(evac, 1)
                    elif j < 12:
                        e.tensor_tensor(by_column(at["kA"][:, j - 9, :]), by_row(b[:]), by_row(rs[:]),
                                        ALU.mult).then_inc(evac, 1)
                    elif j < 15:
                        back = at["qC"][:, j - 12, ::-1].rearrange("p (i n) -> p i n", i=4)[:, ::-1]
                        e.tensor_tensor(back, b[:].rearrange("p (i n) -> p i n", i=4),
                                        rsq[:].rearrange("p (i n) -> p i n", i=4), ALU.mult).then_inc(evac, 1)
                    else:
                        e.tensor_tensor(at["kC"][:, j - 15, :], b[:], rs[:], ALU.mult).then_inc(evac, 1)
                for c in range(HYT):
                    e.wait_ge(hyout, L * 7 + 7)
                    e.wait_ge(ybh, L * 2 + c + 1)
                    e.tensor_tensor(uL[:, 3 + c, :], yb[c][:], uH[:, 3 + c, :].bitcast(F32),
                                    ALU.subtract).then_inc(m_ready, 1)
                low(e, L, U_WO, DT)
                low(e, L, U_WO + 1, DT)
                e.wait_ge(bias_ready, L * 18 + 18)
                attention(L, "A")
                e.wait_ge(c_strip_loaded, L * 16 + 16)
                attention(L, "C")

                def out_tiles(base, a):
                    for j in range(8):
                        if j < 6:
                            low(e, L, base + j + 2, DT)
                        add_square(L, a, j)
                out_tiles(U_WO, 1)
                low(e, L, U_XQ, DT)
                low(e, L, U_XQ + 1, DT)
                boundary(L, 1, xa["yx"])
                for j in range(24):
                    if j < 22:
                        low(e, L, U_XQ + j + 2, DT)
                    if j < 8:
                        e.wait_ge(memh_ready, L * 8 + j + 1)
                        e.scalar_tensor_tensor(xa["memL"][:, j, :], xa["memT"][:, j, :],
                                               pr[:, G0 + G_MEM * 8 + j:G0 + G_MEM * 8 + j + 1],
                                               xa["memH"][:, j, :].bitcast(F32), ALU.mult,
                                               ALU.subtract).then_inc(mem_ready, 1)
                    wait_unit(e, L, U_XQ + j)
                    b = bank[(U_XQ + j) % 4]
                    if j < 8:
                        e.scalar_tensor_tensor(xa["qX"][:, j, :], b[:], -1.0 / 16, rs[:], ALU.mult,
                                               ALU.mult).then_inc(evac, 1)
                    else:
                        dst = xa["kX"][:, j - 8, :] if j < 16 else xa["vX"][:, j - 16, :]
                        e.tensor_tensor(dst, b[:, 0:MEM], rsm[:], ALU.mult).then_inc(evac, 1)
                low(e, L, U_XO, DT)
                low(e, L, U_XO + 1, DT)
                attention(L, "X")
                out_tiles(U_XO, 2)
                low(e, L, U_IN[1], DT)
                low(e, L, U_IN[1] + 1, DT)
                boundary(L, 2, xa["yx"])
                ffn(L, 1)
                post_rs(L, 3)
                for k in range(DT):
                    if k >= 2:
                        e.wait_ge(x_ready, L * 32 + (24 + k - 1 + X0))
                    update(L, 3, k, yf)

        @block.gpsimd
        def _(e):
            e.dma_start(st["memS"][:], mem).then_inc(setup_loaded, 16)
            e.dma_start(st["hot"][0:32, :], k_hot).then_inc(setup_loaded, 16)
            e.dma_start(st["lnn"][0:C_H, :], k_lnn).then_inc(setup_loaded, 16)
            e.dma_start(st["t5s"][0:32, 0:C_H], t5).then_inc(setup_loaded, 16)
            e.dma_start(eye[:], k_eye).then_inc(setup_loaded, 16)
            e.wait_ge(s_t5b, 2)
            e.dma_start(scratch, st["lnn"][0:C_H, :]).then_inc(scratch_out, 16)
            e.wait_ge(scratch_out, 16)
            with e.Fori(0, LAYERS) as L:
                one = bass.ds(L, 1)
                wait_apart(e, x_ready, L * 32 + X0)
                e.dma_start(pr[:], par[one].rearrange("a p n -> (a p) n")).then_inc(params_loaded, 16)
                loads = [(hy["emb"][0:EMB, :], k_emb),
                         (hy["w1"][0:EMB, :], fw1[one].rearrange("a p n -> (a p) n")),
                         (hy["w2"][0:FW, :], fw23[bass.ds(2 * L, 1)].rearrange("a p n -> (a p) n")),
                         (hy["w3"][0:FW, :], fw23[bass.ds(2 * L + 1, 1)].rearrange("a p n -> (a p) n")),
                         (hy["w4"][0:FW, :], fw4[one].rearrange("a p n -> (a p) n")),
                         (hy["fv"][0:FW, 0:4], fvec[one].rearrange("a p n -> (a p) n")),
                         (hy["tneg"][:], k_time),
                         (tmp[0][:], decay[one].to_broadcast([P, 512])),
                         (hy["fwd"][:, 0], k_fwd[0]), (hy["fwd"][:, 1], k_fwd[1]),
                         (hy["inv"][:], k_inv)]
                wait_apart(e, x_ready, L * 32 + (8 + X0))
                for dst, src in loads:
                    e.dma_start(dst, src).then_inc(hy_loaded, 16)
                wait_apart(e, hyout, L * 7 + 4)
                e.dma_start(amask, k_namask).then_inc(strips_loaded, 16)
                for h in range(NA_H):
                    for r in range(WR):
                        e.dma_start(rstrip[r * 16:r * 16 + 16, h],
                                    bass.AP(tensor=rpb.tensor, offset=L * (NA_H * 960) + (h * 960 + r * 64),
                                            ap=[[1, 16], [64, WR], [1, 48]])).then_inc(strips_loaded, 16)
                e.wait_ge(strips_loaded, L * (16 * 49) + 16 * 49)
                for y, c0 in enumerate((16, 8, 0)):
                    for h in range(NA_H):
                        e.tensor_tensor(by_column(at["biasA"][:, y, h, :]), by_column(amask[:, y, :]),
                                        rstrip[:, h, :, c0:c0 + 32], ALU.subtract).then_inc(bias_ready, 1)
                wait_apart(e, bias_ready, L * 18 + 18)
                e.dma_start(strip[:], bass.AP(tensor=scratch.tensor, offset=0,
                                              ap=[[1, P], [1024, C_H], [1, STRIP]])).then_inc(c_strip_loaded, 16)
                wait_apart(e, o_split, L * 32 + 24)
                e.dma_start(xa["memT"][:], mem).then_inc(mem_loaded, 16)


def by_row(ap):
    return ap.rearrange("p (r c) -> p r c", r=ROWS)


def by_column(ap):
    return ap.rearrange("p (c r) -> p r c", r=ROWS)


def oh_per(kind):
    return 1 if kind == "X" else 3


def o_count(kind, g):
    return {"A": 0, "C": 12, "X": 24}[kind] + g * oh_per(kind)


def x_out(t, g):
    i, pair = g // 2, g % 2
    return t[:, 4 * pair:4 * pair + 4, i * P:i * P + P]


def ac_out(t, kind, i, c):
    k = c if kind == "A" else 5 + c
    if kind == "A":
        dst = t[:, k, :].rearrange("p (r i c) -> p r i c", r=ROWS, i=4)[:, :, i, :]
        return dst, lambda b: b[:, c * P:c * P + P][:, ::-1].rearrange("p (r c) -> p r c", r=ROWS), k
    return t[:, k, i * P:i * P + P], lambda b: b[:, c * P:c * P + P][:, ::-1], k


def t5_bucket(rel):
    half, exact = 16, 8
    n = np.abs(rel)
    far = exact + (np.log(np.maximum(n, 1) / exact) / math.log(1024 / exact) * (half - exact)).astype(np.int32)
    far = np.minimum(far, half - 1)
    return np.where(rel > 0, half, 0) + np.where(n < exact, n, far)


def constants():
    f = np.float32
    t = np.linspace(0.0, 1.0, T, dtype=f)
    bands = np.linspace(1e-4, 15, 16, dtype=f)
    ang = (f(2.0 * math.pi / T) * np.arange(T, dtype=f))[:, None] * bands[None, :]
    emb = np.concatenate([t[:, None], np.cos(ang), -np.sin(ang)], 1).astype(f).T.copy()
    kk = 2 * np.pi * (np.arange(T) + 0.5) / (2 * T)
    ph = np.outer(np.arange(T), kk)

    def tiles(a):
        return a.reshape(4, P, T).transpose(1, 0, 2)
    fwd = np.stack([tiles(np.cos(ph)), tiles(np.sin(ph))]).astype(f)
    inv = np.stack([tiles(np.cos(ph).T / T), tiles(np.sin(ph).T / T)], 1).astype(f)
    time = -t.reshape(4, P).T.copy()
    mask = np.full((3, P, 32, WR), BIG, f)
    for y, i in enumerate((0, 1, 3)):
        for c in range(16):
            col = 16 * i + c
            cs = min(max(col - WC // 2, 0), COLS - WC)
            keys = NA_START[i] + np.arange(32)
            ok = (keys >= cs) & (keys < cs + WC)
            for r in range(ROWS):
                mask[y, P - 1 - (r * 16 + c)][:] = np.where(ok[:, None], f(0), f(BIG))
    mask = mask.transpose(1, 0, 2, 3).reshape(P, 3, 256).copy()
    rel = np.arange(1023) - 511
    hot = np.zeros((32, 1024), f)
    hot[t5_bucket(rel), np.arange(1023)] = 1
    count = (np.abs(rel) <= 64).astype(int) + ((rel % 4 == 0) & (np.abs(rel) <= 256)) + (rel % 16 == 0)
    lnn = np.full(1024, BIG, f)
    lnn[:1023] = np.where(count > 0, -np.log(np.maximum(count, 1)), BIG)
    return dict(k_emb=emb, k_fwd=fwd, k_inv=inv, k_time=time, k_namask=mask, k_hot=hot,
                k_lnn=np.tile(lnn, (C_H, 1)), k_eye=np.eye(P, dtype=f))


def columns(w, k):
    lead = w.shape[:-2]
    n = w.shape[-1] // P
    w = w.reshape(*lead, k, P, n, P)
    m = len(lead)
    w = w.transpose(*range(m), m + 2, m + 1, m, m + 3)
    return w.reshape(*lead, n, P, k * P)


def lay_out(i):
    a = {}
    a["x"] = i["x"][0].T.reshape(DT, P, T)
    a["mem"] = i["mem"][0].T.reshape(DT, P, MEM).transpose(1, 0, 2)
    g = i["norm_g"].reshape(LAYERS, 10, DT, P).transpose(0, 3, 1, 2).reshape(LAYERS, P, 80)
    cw = i["hy_conv_w"].reshape(LAYERS, 3, 6, P).transpose(0, 3, 1, 2).reshape(LAYERS, P, 18)
    cb = i["hy_conv_b"].reshape(LAYERS, 6, P).transpose(0, 2, 1)
    sk = i["hy_skip"].reshape(LAYERS, HYT, P).transpose(0, 2, 1)
    a["par"] = np.concatenate([g, cw, cb, sk], -1)
    first = columns(i["ffn_w_in"], DT)
    first = first.reshape(LAYERS, 2, 2, FT, P, D).transpose(0, 1, 3, 2, 4, 5)
    a["w_first"] = first.reshape(LAYERS * 88, P, D)
    second = i["ffn_w_out"].reshape(LAYERS, 2, 2, FH, P, DT, P).transpose(0, 1, 5, 2, 4, 3, 6)
    a["w_second"] = second.reshape(LAYERS * 32, P, FH * P)
    w_in = columns(i["w_in"], DT)
    order = [9, 10, 11, 12, 13, 14, 6, 7, 8, 21, 22, 23, 0, 1, 2, 3, 4, 5, 15, 16, 17, 18, 19, 20]
    a["w_proj"] = np.concatenate([w_in[:, order], columns(i["w_out"], DT), columns(i["xa_wq"], DT),
                                  columns(i["xa_wkv"], DT), columns(i["xa_wo"], DT)], 1
                                 ).reshape(LAYERS * 64, P, D)
    rpb = np.zeros((LAYERS, NA_H, 15, 64), i["na_rpb"].dtype)
    rpb[..., 16:47] = i["na_rpb"]
    a["rpb"] = rpb.reshape(-1)
    a["t5"] = i["t5_table"]
    a["fw1"] = i["hy_f_w1"]
    a["fw23"] = np.stack([i["hy_f_w2"], i["hy_f_w3"]], 1).reshape(LAYERS * 2, FW, FW)
    a["fw4"] = i["hy_f_w4"]
    a["fvec"] = np.stack([i["hy_f_b1"], i["hy_f_b2"], i["hy_f_b3"], i["hy_freq"]], -1)
    a["decay"] = i["hy_decay"]
    return a


ORDER = ("x", "mem", "par", "w_first", "w_second", "w_proj", "rpb", "t5", "fw1", "fw23", "fw4", "fvec", "decay",
         "k_emb", "k_fwd", "k_inv", "k_time", "k_namask", "k_hot", "k_lnn", "k_eye")


def kernel(**inputs):
    import concourse.bacc as bacc
    from concourse.bass_utils import run_bass_kernel_spmd

    nc = bacc.Bacc("TRN2", target_bir_lowering=False, num_devices=1)
    data = lay_out({k: np.asarray(v) for k, v in inputs.items()})
    data.update(constants())
    arrays, args = {}, []
    for name in ORDER:
        a = np.ascontiguousarray(data[name])
        arrays["in_" + name] = a
        args.append(nc.dram_tensor("in_" + name, a.shape, mybir.dt.from_np(a.dtype), kind="ExternalInput").ap())
    args.append(nc.dram_tensor("out_x", (DT, P, T), F32, kind="ExternalOutput").ap())
    build(nc, *args)
    got = run_bass_kernel_spmd(nc, [arrays], core_ids=[0])
    return np.ascontiguousarray(got.results[0]["out_x"].reshape(D, T).T[None])
```

```python
from contextlib import ExitStack
import math

import numpy as np
import concourse.bass as bass
from concourse import mybir

ALU = mybir.AluOpType
ACT = mybir.ActivationFunctionType
F32 = mybir.dt.float32
F32R = mybir.dt.float32r
AX = mybir.AxisListType

P = 128
LAYERS = 2
D = 1024
T = 512
DT = D // P
MEM = 256
MT = MEM // P
KVW = 512
FF = 2816
FT = FF // P
FH = FT // 2
EPS = 1e-6
ROWS, COLS = 8, 64
NA_H = 6
WC, WR = 16, 8
C_H = 6
HYT = 2
FW = 64
EMB = 33
BIG = 1e30
KEEP_BUSY = 3
LOG_EXP_SET = 6
STRIP = 7 * P

U_IN = (0, 124)
U_OUT = (44, 168)
U_HY, U_VA, U_VC, U_QA, U_KA, U_QC, U_KC = 60, 66, 69, 72, 75, 78, 81
U_WO, U_XQ, U_XK, U_XV, U_XO = 84, 92, 100, 108, 116
UNITS = 184
USED0, SPLIT0, EVAC0, X0 = 2, 4, 4, 1
IT_A, IT_C, IT_X, ITEMS = 0, 24, 48, 64
GR_A, GR_C, GR_X, GROUPS = 0, 4, 8, 16

TWO_PI_HI = 6.28125
TWO_PI_LO = 2 * math.pi - TWO_PI_HI
ROUND = 1.5 * 2.0 ** 23
PI_IN = 3.1415925
G0, CW0, CB0, SK0, NPAR = 0, 80, 98, 104, 106
PRE = (0, 2, 5, 8)
POST = (1, 4, 7, 9)
G_GROUP, G_MEM = 3, 6
NA_START = (0, 8, 24, 32)
NA_CHUNKS = (0, 8, 16, 24, 32, 40, 48)


def build(nc, x, mem, par, w_first, w_second, w_proj, rpb, t5, fw1, fw23, fw4, fvec, decay,
          k_emb, k_fwd, k_inv, k_time, k_namask, k_hot, k_lnn, k_eye, out):
    with ExitStack() as ctx:
        def sb(name, shape, dt=F32):
            return ctx.enter_context(nc.sbuf_tensor(name, shape, dt))

        def sem(name):
            return ctx.enter_context(nc.semaphore(name))

        bank = [ctx.enter_context(nc.psum_tensor(f"bank{i}", [P, 512], F32)) for i in range(8)]

        xT = sb("xT", [P, DT, T])
        raw = [sb(f"raw{i}", [P, FH * P]) for i in range(4)]
        wh = [sb(f"wh{i}", [P, FH * P], F32R) for i in range(2)]
        wl = [sb(f"wl{i}", [P, FH * P], F32R) for i in range(2)]
        rs = sb("rs", [P, T])
        rsq = sb("rsq", [P, T])
        rsp = sb("rsp", [P, T])
        rsm = sb("rsm", [P, MT])
        tmp = [sb(f"tmp{i}", [P, T]) for i in range(6)]
        yb = [sb(f"yb{i}", [P, T]) for i in range(HYT)]
        ones = sb("ones", [P, P])
        eye = sb("eye", [P, P])
        epsc = sb("epsc", [P, 2])
        pr = sb("pr", [P, NPAR])
        negmax = sb("negmax", [P, ITEMS])
        den = sb("den", [P, ITEMS])
        rden = sb("rden", [P, ITEMS])
        gss = sb("gss", [P, 3, GROUPS])

        def overlay(*sets):
            return [over(s) for s in sets]

        base = nc.sbuf_base if not callable(nc.sbuf_base) else nc.sbuf_base()

        def place(parts):
            made = {}
            with ExitStack() as st:
                for name, shape, dt in parts:
                    made[name] = st.enter_context(nc.sbuf_tensor(name, shape, dt))
            return made

        yf = place([("yf", [P, DT, T], F32)])["yf"]
        uH = sb("uH", [P, DT, T], F32R)
        uL = sb("uL", [P, DT, T], F32R)
        hid = place([("hH", [P, FT * T], F32R), ("hL", [P, FT * T], F32R)])
        hH, hL = hid["hH"], hid["hL"]
        hy = place([
            ("p", [P, 6, T + 2], F32), ("uc", [P, 6, T], F32), ("fwd", [P, 2, 4, T], F32),
            ("inv", [P, 2, 4, T], F32), ("filt", [P, 2, 4, 256], F32), ("taps", [P, 4, 512], F32),
            ("even", [P, 4, 256], F32), ("zt", [P, 4, 256], F32), ("emb", [P, T], F32),
            ("w1", [P, FW], F32), ("w2", [P, FW], F32), ("w3", [P, FW], F32), ("w4", [P, 512], F32),
            ("fv", [P, 8], F32), ("tneg", [P, 4], F32)])
        at = place([
            ("qA", [P, 3, T], F32), ("kA", [P, 3, T], F32), ("vt", [P, 3, T], F32),
            ("VA", [P, 7, 384], F32), ("biasA", [P, 3, NA_H, 256], F32), ("qC", [P, 3, T], F32),
            ("kC", [P, 3, T], F32), ("VC", [P, 4, 384], F32), ("strip", [P, C_H, STRIP], F32)])
        ac = place([
            ("over_qA", [P, 3, T], F32), ("over_kA", [P, 3, T], F32), ("kCh", [P, 3, T], F32R),
            ("over_VA", [P, 7, 384], F32), ("qCh", [P, 3, T], F32R), ("over_biases", [P, 2, NA_H, 256], F32),
            ("qCl", [P, 3, T], F32R), ("kCl", [P, 3, T], F32R)])
        xa = place([
            ("memT", [P, DT, MEM], F32), ("memH", [P, DT, MEM], F32R), ("memL", [P, DT, MEM], F32R),
            ("qX", [P, DT, T], F32), ("kX", [P, DT, MEM], F32), ("kT", [P, MT, D], F32),
            ("VX", [P, MT, D], F32), ("yx", [P, DT, T], F32)])
        st = place([("hot", [P, 1024], F32), ("lnn", [P, 1024], F32),
                    ("t5s", [P, 8], F32)])
        strip = at["strip"]
        rstrip = strip[:].rearrange("p h n -> p (h n)")[:, 0:NA_H * 384].rearrange(
            "p (h r c) -> p h r c", h=NA_H, r=WR)
        amask = strip[:].rearrange("p h n -> p (h n)")[:, NA_H * 384:NA_H * 384 + 768].rearrange(
            "p (y n) -> p y n", y=3)
        scratch = nc.dram_tensor("bias_of_distance", (C_H, 1024), F32, kind="Internal").ap()
        region = ctx.enter_context(nc.sbuf_tensor("region", [P, 2 * FT * T], F32))
        assert region is not None
        on = sb("on", [P, T])

        params_loaded = sem("params_loaded")
        setup_loaded = sem("setup_loaded")
        x_loaded = sem("x_loaded")
        landed = [sem(f"landed{i}") for i in range(4)]
        high_ready = sem("high_ready")
        split_ready = sem("split_ready")
        unit_done = sem("unit_done")
        evac = sem("evac")
        const_set = sem("const_set")
        x_ready = sem("x_ready")
        uh_ready = sem("uh_ready")
        u_ready = sem("u_ready")
        presq = sem("presq")
        preacc = sem("preacc")
        presum = sem("presum")
        prelog = sem("prelog")
        rs_ready = sem("rs_ready")
        rsq_ready = sem("rsq_ready")
        postsq = sem("postsq")
        postacc = sem("postacc")
        postsum = sem("postsum")
        postlog = sem("postlog")
        rsp_ready = sem("rsp_ready")
        y_scaled = sem("y_scaled")
        gate_scaled = sem("gate_scaled")
        silu_ready = sem("silu_ready")
        hid_ready = sem("hid_ready")
        hidh_ready = sem("hidh_ready")
        hid_split = sem("hid_split")
        hy_small = sem("hy_small")
        hy_loaded = sem("hy_loaded")
        inv_loaded = sem("inv_loaded")
        pad_zero = sem("pad_zero")
        conv = sem("conv")
        z_ready = sem("z_ready")
        f_mm = sem("f_mm")
        f_arg = sem("f_arg")
        f_red = sem("f_red")
        f_sin = sem("f_sin")
        f_bias = sem("f_bias")
        taps_mm = sem("taps_mm")
        absd = sem("absd")
        window = sem("window")
        taps_ready = sem("taps_ready")
        filt_mm = sem("filt_mm")
        filt_ready = sem("filt_ready")
        zt_mm = sem("zt_mm")
        zt_ready = sem("zt_ready")
        z_mm = sem("z_mm")
        prod = sem("prod")
        y_mm = sem("y_mm")
        hyout = sem("hyout")
        hysq = sem("hysq")
        hysum = sem("hysum")
        hylog = sem("hylog")
        ybh = sem("ybh")
        m_ready = sem("m_ready")
        strips_loaded = sem("strips_loaded")
        bias_ready = sem("bias_ready")
        c_strip_loaded = sem("c_strip_loaded")
        c_high = sem("c_high")
        c_split = sem("c_split")
        vt_mm = sem("vt_mm")
        vt_out = sem("vt_out")
        score_mm = sem("score_mm")
        biased = sem("biased")
        prob_ready = sem("prob_ready")
        pt_mm = sem("pt_mm")
        pt_ready = sem("pt_ready")
        pv_mm = sem("pv_mm")
        rden_ready = sem("rden_ready")
        o_read = sem("o_read")
        g_sq = sem("g_sq")
        g_log = sem("g_log")
        hyrs = sem("hyrs")
        g_rs = sem("g_rs")
        o_ready = sem("o_ready")
        ot_mm = sem("ot_mm")
        oh_ready = sem("oh_ready")
        o_split = sem("o_split")
        mem_loaded = sem("mem_loaded")
        memh_ready = sem("memh_ready")
        mem_ready = sem("mem_ready")
        kt_mm = sem("kt_mm")
        kt_out = sem("kt_out")
        s_mact = sem("s_mact")
        s_msq = sem("s_msq")
        s_mmm = sem("s_mmm")
        mem_log = sem("mem_log")
        rsm_ready = sem("rsm_ready")
        s_t5 = sem("s_t5")
        s_t5b = sem("s_t5b")
        scratch_out = sem("scratch_out")
        stored = sem("stored")
        passed = sem("passed")

        def wait_apart(e, sem_, value):
            e.wait_ge(sem_, value).then_inc(passed, 1)

        def wait_unit(e, L, u):
            e.wait_ge(unit_done, L * UNITS + u + 1 + USED0)

        def high(e, L, u, k, it=0):
            e.wait_ge(landed[u % 4], (L * (UNITS // 4) + (u // 4 + 1) + it) * 16)
            e.wait_ge(unit_done, L * UNITS + 4 * it + (u - 1 + USED0))
            e.activation(wh[u % 2][:, 0:k * P], raw[u % 4][:, 0:k * P], ACT.Copy).then_inc(high_ready, 1)

        def low(e, L, u, k, it=0):
            e.wait_ge(high_ready, L * UNITS + 4 * it + (u + 1))
            e.tensor_tensor(wl[u % 2][:, 0:k * P], raw[u % 4][:, 0:k * P],
                            wh[u % 2][:, 0:k * P].bitcast(F32), ALU.subtract).then_inc(split_ready, 1)

        block = ctx.enter_context(nc.Block())

        @block.sync
        def _(e):
            def load(L, u, src, k, it=0):
                e.wait_ge(split_ready, L * UNITS + 4 * it + (u - 3 + SPLIT0))
                e.dma_start(raw[u % 4][:, 0:k * P], src).then_inc(landed[u % 4], 16)

            for k in range(DT):
                e.dma_start(xT[:, k, :], x[k]).then_inc(x_loaded, 16)
            with e.Fori(0, LAYERS) as L:
                def ffn(f):
                    with e.Fori(0, FT // 2) as it:
                        for j in range(4):
                            load(L, U_IN[f] + j, w_first[bass.ds(L * 88 + it * 4 + (f * 44 + j), 1)].rearrange(
                                "a p n -> (a p) n"), DT, it)
                    with e.Fori(0, 4) as it:
                        for j in range(4):
                            load(L, U_OUT[f] + j, w_second[bass.ds(L * 32 + it * 4 + (f * 16 + j), 1)].rearrange(
                                "a p n -> (a p) n"), FH, it)

                ffn(0)
                with e.Fori(0, 16) as it:
                    for j in range(4):
                        load(L, U_HY + j, w_proj[bass.ds(L * 64 + it * 4 + j, 1)].rearrange(
                            "a p n -> (a p) n"), DT, it)
                ffn(1)
            for k in range(DT):
                e.wait_ge(x_ready, LAYERS * 32 - 7 + k + X0)
                e.dma_start(out[k], xT[:, k, :]).then_inc(stored, 16)
            e.wait_ge(stored, 16 * DT)

        @block.tensor
        def _(e):
            def unit(L, u, k, rH, rL, it=0, dest=None, first=True, last=True, n=T, k0=0):
                b = bank[u % 4 if dest is None else dest]
                e.wait_ge(split_ready, L * UNITS + 4 * it + (u + 1 + SPLIT0))
                if first:
                    e.wait_ge(evac, L * UNITS + 4 * it + (u - 3 + EVAC0))
                for kk in range(k):
                    cut = slice(kk * P, kk * P + P)
                    e.matmul(b[:, 0:n], wh[u % 2][:, cut], rH(k0 + kk), start=first and kk == 0, stop=False)
                    e.matmul(b[:, 0:n], wh[u % 2][:, cut], rL(k0 + kk), start=False, stop=False)
                    mm = e.matmul(b[:, 0:n], wl[u % 2][:, cut], rH(k0 + kk), start=False,
                                  stop=last and kk == k - 1)
                mm.then_inc(unit_done, 1)

            def memory_unit(L, j):
                u, block, part = U_XK + j, j // 4, j % 4
                e.wait_ge(split_ready, L * UNITS + (u + 1 + SPLIT0))
                if part == 0:
                    e.wait_ge(evac, L * UNITS + (u - (4 if block else 2) + EVAC0))
                for m in range(MT):
                    b = bank[2 * (block % 2) + m]
                    for kk in range(2):
                        k = 2 * part + kk
                        hi, lo = (xa[n][:, k, m * P:m * P + P] for n in ("memH", "memL"))
                        cut = slice(kk * KVW, kk * KVW + KVW)
                        e.matmul(b[:], hi, wh[u % 2][:, cut], start=k == 0, stop=False)
                        e.matmul(b[:], hi, wl[u % 2][:, cut], start=False, stop=False)
                        mm = e.matmul(b[:], lo, wh[u % 2][:, cut], start=False, stop=k == DT - 1)
                mm.then_inc(unit_done, 1)

            def u_of(k):
                return uH[:, k, :]

            def ul_of(k):
                return uL[:, k, :]

            def first_units(L, u, a):
                for n in range(2):
                    e.wait_ge(split_ready, L * UNITS + (u + n + 1 + SPLIT0))
                    e.wait_ge(evac, L * UNITS + (u + n - 3 + EVAC0))
                for k in range(DT):
                    e.wait_ge(u_ready, L * 32 + (a * 8 + k + 1))
                    cut = slice(k * P, k * P + P)
                    for n in range(2):
                        b, w = bank[(u + n) % 4], (u + n) % 2
                        e.matmul(b[:], wh[w][:, cut], uH[:, k, :], start=k == 0, stop=False)
                        e.matmul(b[:], wh[w][:, cut], uL[:, k, :], start=False, stop=False)
                        mm = e.matmul(b[:], wl[w][:, cut], uH[:, k, :], start=False, stop=k == DT - 1)
                        if k == DT - 1:
                            mm.then_inc(unit_done, 1)

            def presum_mm(L, a):
                e.wait_ge(preacc, L * 32 + (a * 8 + DT))
                e.matmul(bank[6][:], ones[:], tmp[3][:], start=True, stop=True).then_inc(presum, 1)

            def postsum_mm(L, a):
                e.wait_ge(postacc, L * 32 + (a * 8 + DT))
                e.matmul(bank[7][:], ones[:], tmp[0][:], start=True, stop=True).then_inc(postsum, 1)

            def ffn(L, f):
                first_units(L, U_IN[f], 3 * f)
                unit(L, U_IN[f] + 2, DT, u_of, ul_of)
                presum_mm(L, 3 * f)
                unit(L, U_IN[f] + 3, DT, u_of, ul_of)
                with e.Fori(1, FT // 2) as it:
                    for j in range(4):
                        unit(L, U_IN[f] + j, DT, u_of, ul_of, it)
                with e.Fori(0, 4) as it:
                    for j in range(4):
                        e.wait_ge(hid_split, L * 44 + (f * 22 + (FH if j == 0 else FT)))
                        unit(L, U_OUT[f] + j, FH, lambda k: hH[:, k * T:k * T + T], lambda k: hL[:, k * T:k * T + T],
                             it, dest=j // 2 * 2, first=j % 2 == 0, last=j % 2 == 1, k0=j % 2 * FH)
                postsum_mm(L, 3 * f)

            def attention(L, part, steps):
                first, n, g0 = (IT_A, 48, GR_A) if part == "mixer" else (IT_X, 16, GR_X)
                per = 2 if part == "cross" else 6
                turn = 5 if part == "cross" else 6

                def ih(t):
                    return (t // 6 % 4, t % 6) if t < IT_X else ((t - IT_X) // 4, t % 4)

                for s in steps:
                    if s < n:
                        t = first + s
                        kind, (i, h) = kind_of(t), ih(t)
                        if part == "mixer" and s < 2:
                            e.wait_ge(evac, L * UNITS + (U_KC + s + EVAC0))
                        if kind == "C" and s == IT_C:
                            e.wait_ge(c_split, L * 6 + 6)
                        if s >= 2:
                            e.wait_ge(prob_ready, L * ITEMS + (t - 1))
                        S = bank[t % 2]
                        if kind == "X":
                            for c in range(2):
                                mm = e.matmul(S[:, 0:MEM], xa["qX"][:, 2 * h + c, i * P:i * P + P],
                                              xa["kX"][:, 2 * h + c, :], start=c == 0, stop=c == 1)
                        else:
                            lo, j = h % 2 * 64, h // 2
                            cut = slice(i * P, i * P + P)
                            if kind == "A":
                                c0 = NA_START[i]
                                mm = e.matmul(S[:, 0:256], at["qA"][lo:lo + 64, j, cut],
                                              at["kA"][lo:lo + 64, j, c0 * ROWS:c0 * ROWS + 256],
                                              start=True, stop=True)
                            else:
                                qh, ql, kh, kl = (ac[x] for x in ("qCh", "qCl", "kCh", "kCl"))
                                e.matmul(S[:], qh[lo:lo + 64, j, cut], kh[lo:lo + 64, j, :], start=True, stop=False)
                                e.matmul(S[:], qh[lo:lo + 64, j, cut], kl[lo:lo + 64, j, :], start=False, stop=False)
                                mm = e.matmul(S[:], ql[lo:lo + 64, j, cut], kh[lo:lo + 64, j, :],
                                              start=False, stop=True)
                        mm.then_inc(score_mm, 1)
                    if part == "mixer" and 2 <= s < 7:
                        for _ in range(KEEP_BUSY):
                            e.matmul(bank[7][:], wh[1][:, 0:P], wh[1][:, 0:T], start=True, stop=True)
                    s2 = s - 2
                    if 0 <= s2 < n:
                        t = first + s2
                        if part == "mixer" and s2 < 2:
                            e.wait_ge(evac, L * UNITS + (U_KC + 2 + s2 + EVAC0))
                        e.wait_ge(prob_ready, L * ITEMS + (t + 1))
                        if s2 >= 2:
                            e.wait_ge(pt_ready, L * ITEMS + (t - 1))
                        for c in range(chunks_of(t)):
                            mm = e.transpose(bank[2 + t % 2][:, c * P:c * P + P],
                                             tmp[t % 4][:, c * P:c * P + P], eye[:])
                        mm.then_inc(pt_mm, 1)
                    s3 = s - 3
                    if 0 <= s3 < n:
                        t = first + s3
                        kind, (i, h) = kind_of(t), ih(t)
                        chunks = chunks_of(t)
                        g = g0 + s3 // per
                        if part == "mixer" and s3 % per:
                            e.matmul(bank[4 + g % 2][:, 384:512], ones[:], eye[:], start=True, stop=True)
                        e.wait_ge(pt_ready, L * ITEMS + (t + 1))
                        if s3 % per == 0 and s3 // per >= 2:
                            e.wait_ge(o_read, L * GROUPS + (g - 1))
                        O = bank[4 + g % 2]
                        w = 256 if kind == "X" else 64
                        col = s3 % per * w
                        for c in range(chunks):
                            if kind == "X":
                                v = xa["VX"][:, c, h * 256:h * 256 + 256]
                            elif kind == "A":
                                v = at["VA"][:, NA_START[i] // 8 + 2 * c, h * 64:h * 64 + 64]
                            else:
                                v = at["VC"][:, c, h * 64:h * 64 + 64]
                            mm = e.matmul(O[:, col:col + w], tmp[4 + t % 2][:, c * P:c * P + P], v,
                                          start=c == 0, stop=c == chunks - 1)
                        mm.then_inc(pv_mm, 1)
                    s5 = s - turn
                    if 0 <= s5 < n and s5 % per == per - 1:
                        g = g0 + s5 // per
                        e.wait_ge(o_ready, L * GROUPS + (g + 1))
                        if s5 // per >= 2:
                            e.wait_ge(o_split, L * 32 + splits_before(g - 1))
                        w = 4 if part == "cross" else 3
                        for c in range(w):
                            mm = e.transpose(bank[6 + g % 2][:, c * P:c * P + P], on[:, c * P:c * P + P], eye[:])
                        mm.then_inc(ot_mm, 1)

            e.wait_ge(const_set, 1)
            e.wait_ge(setup_loaded, 16 * 4)
            for c in range(2):
                e.matmul(bank[c][0:C_H, :], st["t5s"][0:32, 0:C_H], st["hot"][0:32, c * T:c * T + T],
                         start=True, stop=True).then_inc(s_t5, 1)
            e.wait_ge(s_t5b, 2)
            e.sem_inc(unit_done, USED0)

            with e.Fori(0, LAYERS) as L:
                ffn(L, 0)

                first_units(L, U_HY, 1)
                for j in range(2, 6):
                    unit(L, U_HY + j, DT, u_of, ul_of)
                    if j == 2:
                        presum_mm(L, 1)
                        wait_apart(e, hy_small, L * 112 + 112)
                        e.matmul(bank[4][0:FW, :], hy["w1"][0:EMB, :], hy["emb"][0:EMB, :], start=True,
                                 stop=True).then_inc(f_mm, 1)
                    elif j <= 4:
                        wait_apart(e, f_sin, L * 3 + j - 2)
                        e.matmul(bank[4][0:FW, :], hy[f"w{j - 1}"][0:FW, :], tmp[3][0:FW, :], start=True,
                                 stop=True).then_inc(f_mm, 1)
                    else:
                        e.wait_ge(f_sin, L * 3 + 3)
                        for m in range(4):
                            e.matmul(bank[4 + m][:], tmp[3][0:FW, m * P:m * P + P], hy["w4"][0:FW, :],
                                     start=True, stop=True).then_inc(taps_mm, 1)
                for half in range(2):
                    e.wait_ge(z_ready, L * 2 + 2)
                    e.wait_ge(taps_ready, L * 7 + half + 1)
                    for tt in (2 * half, 2 * half + 1):
                        for c in range(HYT):
                            mm = e.transpose(bank[4 + half][:, (tt % 2 * 2 + c) * P:(tt % 2 * 2 + c) * P + P],
                                             hy["uc"][:, c, tt * P:tt * P + P], eye[:])
                    mm.then_inc(zt_mm, 1)
                e.wait_ge(taps_ready, L * 7 + 7)
                e.wait_ge(hy_loaded, L * 48 + 48)
                e.wait_ge(zt_ready, L * 2 + 2)
                for part in range(2):
                    for half in range(2):
                        for kt in (2 * half, 2 * half + 1):
                            for m in range(4):
                                rhs = hy["even"][:, m, :] if part == 0 else hy["taps"][:, m, 256:512]
                                mm = e.matmul(bank[4 + 2 * part + half][:, kt % 2 * 256:kt % 2 * 256 + 256],
                                              hy["fwd"][:, part, m, kt * P:kt * P + P], rhs,
                                              start=m == 0, stop=m == 3)
                        mm.then_inc(filt_mm, 1)
                e.wait_ge(filt_ready, L * 4 + 4)
                for part in range(2):
                    for half in range(2):
                        for kt in (2 * half, 2 * half + 1):
                            for m in range(4):
                                mm = e.matmul(bank[6 - 2 * part + half][:, kt % 2 * 256:kt % 2 * 256 + 256],
                                              hy["fwd"][:, part, m, kt * P:kt * P + P], hy["zt"][:, m, :],
                                              start=m == 0, stop=m == 3)
                        mm.then_inc(z_mm, 1)
                e.wait_ge(prod, L * 12 + 12)
                e.wait_ge(inv_loaded, L * 16 + 16)
                for c in range(HYT):
                    for part in range(2):
                        for kt in range(4):
                            mm = e.matmul(bank[4 + c][:], hy["taps"][:, kt, part * 256 + c * P:part * 256 + c * P + P],
                                          hy["inv"][:, part, kt, :], start=part + kt == 0, stop=part == 1 and kt == 3)
                    mm.then_inc(y_mm, 1)
                for c in range(HYT):
                    e.wait_ge(hysq, L * 2 + c + 1)
                    mm = e.matmul(bank[6][:], ones[:], tmp[4 + c][:], start=c == 0, stop=c == 1)
                mm.then_inc(hysum, 1)

                def turn_values(j):
                    e.wait_ge(evac, L * UNITS + (U_VA + j + 1 + EVAC0))
                    vt = at["vt"][:, j % 3, :]
                    if j < 3:
                        for half in range(2):
                            if j >= 1:
                                e.wait_ge(vt_out, L * 9 + 2 * j - 1 + half)
                            for n, c in enumerate(NA_CHUNKS[4 * half:4 * half + 4]):
                                mm = e.transpose(bank[4 + half][:, n * P:n * P + P], vt[:, c * ROWS:c * ROWS + P], eye[:])
                            mm.then_inc(vt_mm, 1)
                    else:
                        b = (4, 5, 4)[j - 3]
                        e.wait_ge(vt_out, L * 9 + (5, 6, 7)[j - 3])
                        for n in range(4):
                            mm = e.transpose(bank[b][:, n * P:n * P + P], vt[:, n * P:n * P + P], eye[:])
                        mm.then_inc(vt_mm, 1)

                for j in range(18):
                    unit(L, U_VA + j, DT, u_of, ul_of)
                    if 1 <= j <= 6:
                        turn_values(j - 1)
                    if j in (15, 16):
                        attention(L, "mixer", [j - 15])
                e.wait_ge(vt_out, L * 9 + 9)
                attention(L, "mixer", range(2, 55))
                e.wait_ge(m_ready, L * 2 + 2)
                e.wait_ge(o_split, L * 32 + 24)
                for j in range(8):
                    unit(L, U_WO + j, DT, u_of, ul_of)
                postsum_mm(L, 1)

                first_units(L, U_XQ, 2)
                for j in range(2, 8):
                    unit(L, U_XQ + j, DT, u_of, ul_of)
                    if j == 2:
                        presum_mm(L, 2)
                    if j == 4:
                        e.wait_ge(s_msq, L * 16 + 16)
                        for m in range(MT):
                            mm = e.matmul(bank[7][:, m:m + 1], tmp[2][:, m * P:m * P + P], ones[:, 0:1],
                                          start=True, stop=True)
                        mm.then_inc(s_mmm, 1)
                e.wait_ge(mem_ready, L * 8 + 8)
                for j in range(16):
                    memory_unit(L, j)
                    if j >= 8 and j % 2 == 1:
                        n = (j - 9) // 2
                        if n == 0:
                            e.wait_ge(evac, L * UNITS + (U_XV + EVAC0))
                        if n >= 2:
                            e.wait_ge(kt_out, L * 4 + n - 1)
                        for c in range(2):
                            for m in range(MT):
                                at_ = c * MEM + m * P
                                mm = e.transpose(bank[4 + n % 2][:, at_:at_ + P],
                                                 xa["kT"][:, m, (2 * n + c) * P:(2 * n + c) * P + P], eye[:])
                        mm.then_inc(kt_mm, 1)
                e.wait_ge(kt_out, L * 4 + 4)
                e.wait_ge(evac, L * UNITS + (U_XO + EVAC0))
                attention(L, "cross", range(22))
                e.wait_ge(o_split, L * 32 + 32)
                for j in range(8):
                    unit(L, U_XO + j, DT, u_of, ul_of)
                postsum_mm(L, 2)
                ffn(L, 1)

        @block.scalar
        def _(e):
            def load_log_exp():
                e.add_instruction(mybir.InstLoadActFuncSet(act_func_set_id=LOG_EXP_SET, ins=[], outs=[],
                                                           name=nc.get_next_instruction_name()))

            def prenorm(L, a, u):
                for k in range(DT):
                    e.wait_ge(x_ready, L * 32 + ((a * 8 - 7 + k if a else 0) + X0))
                    e.activation(uH[:, k, :], xT[:, k, :], ACT.Copy,
                                 scale=pr[:, G0 + PRE[a] * 8 + k:G0 + PRE[a] * 8 + k + 1]).then_inc(uh_ready, 1)
                for k in range(DT):
                    if k >= 2:
                        e.wait_ge(preacc, L * 32 + (a * 8 + k - 1))
                    e.activation(tmp[4 + k % 2][:], xT[:, k, :], ACT.Square).then_inc(presq, 1)
                    if k == 1:
                        high(e, L, u + 2, DT)
                high(e, L, u + 3, DT)

            def pre_rs(L, a):
                e.wait_ge(presum, L * 4 + (a + 1))
                e.activation(rs[:], bank[6][:], ACT.Ln, scale=1.0 / D, bias=epsc[:, 0:1]).then_inc(prelog, 1)
                e.wait_ge(prelog, L * 4 + (a + 1))
                e.activation(rs[:], rs[:], ACT.Exp, scale=-0.5).then_inc(rs_ready, 1)

            def post_rs(L, a):
                half = a in (0, 3)
                e.wait_ge(postsum, L * 4 + (a + 1))
                e.activation(rsp[:], bank[7][:], ACT.Ln, scale=(4.0 if half else 1.0) / D,
                             bias=epsc[:, 1:2] if half else epsc[:, 0:1]).then_inc(postlog, 1)
                e.wait_ge(postlog, L * 4 + (a + 1))
                e.activation(rsp[:], rsp[:], ACT.Exp, scale=-0.5).then_inc(rsp_ready, 1)

            def y_tile(L, a, j, src, dst, inc, it=None):
                k = j if it is None else 2 * it + j
                if it is None and j >= 2:
                    e.wait_ge(postacc, L * 32 + (a * 8 + j - 1))
                e.activation(tmp[4 + j % 2][:], src[:], ACT.Square).then_inc(postsq, 1)
                e.activation(dst, src[:], ACT.Copy).then_inc(evac, inc)

            def ffn(L, f):
                a = 3 * f
                if f == 0:
                    e.wait_ge(params_loaded, L * 16 + 16)
                    high(e, L, U_IN[0], DT)
                    high(e, L, U_IN[0] + 1, DT)
                    prenorm(L, 0, U_IN[0])
                pre_rs(L, a)
                def pair(q, it, ahead):
                    p = L * 44 + 2 * it + (f * 22 + q)
                    if ahead:
                        high(e, L, U_IN[f] + 2 * q + 2, DT, it)
                    e.wait_ge(gate_scaled, p + 1)
                    e.activation(tmp[q][:], tmp[q][:], ACT.Silu).then_inc(silu_ready, 1)
                    if ahead:
                        high(e, L, U_IN[f] + 2 * q + 3, DT, it)
                    e.wait_ge(hid_ready, p + 1)
                    e.activation(hH[:, bass.ds((2 * it + q) * T, T)], tmp[2 + q][:], ACT.Copy).then_inc(hidh_ready, 1)
                pair(0, 0, False)
                pair(1, 0, True)
                with e.Fori(1, FT // 2 - 1) as it:
                    pair(0, it, True)
                    pair(1, it, True)
                last = FT // 2 - 1
                pair(0, last, True)
                high(e, L, U_OUT[f], FH)
                pair(1, last, False)
                high(e, L, U_OUT[f] + 1, FH)
                load_log_exp()

                def tile(q, it, ahead):
                    u = U_OUT[f] + 2 * q
                    if ahead:
                        high(e, L, u + 2, FH, it)
                        high(e, L, u + 3, FH, it)
                    else:
                        e.wait_ge(unit_done, L * UNITS + 4 * it + (u + 2 + USED0))
                    e.wait_ge(postacc, L * 32 + 2 * it + (a * 8 + q - 1)) if not (isinstance(it, int) and it == 0) else None
                    e.activation(tmp[4 + q][:], bank[2 * q][:], ACT.Square).then_inc(postsq, 1)
                    e.activation(yf[:, bass.ds(2 * it + q, 1), :].rearrange("p a n -> p (a n)"), bank[2 * q][:],
                                 ACT.Copy).then_inc(evac, 2)
                tile(0, 0, True)
                tile(1, 0, True)
                with e.Fori(1, 3) as it:
                    tile(0, it, True)
                    tile(1, it, True)
                tile(0, 3, True)
                tile(1, 3, False)
                post_rs(L, a)

            def attention(L, part, steps):
                first, n, g0 = (IT_A, 48, GR_A) if part == "mixer" else (IT_X, 16, GR_X)
                per = 2 if part == "cross" else 6
                turn = 5 if part == "cross" else 6
                for s in steps:
                    if s < n:
                        t = first + s
                        kind, wide = kind_of(t), chunks_of(t) * P
                        e.wait_ge(biased, L * ITEMS + (t + 1))
                        if kind == "X" and s >= 4:
                            e.wait_ge(pt_mm, L * ITEMS + (t - 3))
                        src = bank[t % 2][:, 0:wide] if kind == "X" else tmp[t % 4][:, 0:wide]
                        e.activation(tmp[t % 4][:, 0:wide], src, ACT.Exp, scale=-1.0, bias=negmax[:, t:t + 1],
                                     accum_out=den[:, t:t + 1]).then_inc(prob_ready, 1)
                    s2 = s - 2
                    if 0 <= s2 < n:
                        t = first + s2
                        wide = chunks_of(t) * P
                        e.wait_ge(pt_mm, L * ITEMS + (t + 1))
                        if s2 >= 2:
                            e.wait_ge(pv_mm, L * ITEMS + (t - 1))
                        e.activation(tmp[4 + t % 2][:, 0:wide], bank[2 + t % 2][:, 0:wide],
                                     ACT.Copy).then_inc(pt_ready, 1)
                    s4 = s - 4
                    if part == "mixer" and 0 <= s4 < n and s4 % per == per - 1:
                        g = g0 + s4 // per
                        e.wait_ge(g_sq, L * 8 + (g + 1))
                        e.activation(gss[:, 1, g:g + 1], gss[:, 0, g:g + 1], ACT.Ln, scale=1.0 / 384,
                                     bias=epsc[:, 0:1]).then_inc(g_log, 1)
                        e.wait_ge(g_log, L * 8 + (g + 1))
                        e.activation(gss[:, 2, g:g + 1], gss[:, 1, g:g + 1], ACT.Exp, scale=-0.5).then_inc(g_rs, 1)
                    s5 = s - turn
                    if 0 <= s5 < n and s5 % per == per - 1:
                        g = g0 + s5 // per
                        e.wait_ge(ot_mm, L * GROUPS + (g + 1))
                        kind = kind_of(first + s5)
                        if kind == "X":
                            dst, src = x_out(uH, g - GR_X), bank[6 + g % 2][:].rearrange("p (c n) -> p c n", c=4)
                            e.activation(dst, src, ACT.Copy).then_inc(oh_ready, 1)
                        else:
                            for c in range(3):
                                dst, src, k = ac_out(uH, kind, g % 4, c)
                                e.activation(dst, src(bank[6 + g % 2]), ACT.Copy,
                                             scale=pr[:, G0 + G_GROUP * 8 + k:G0 + G_GROUP * 8 + k + 1]
                                             ).then_inc(oh_ready, 1)
                    if part == "mixer":
                        if s in (26, 30):
                            high(e, L, U_WO + (s - 26) // 4, DT)
                        if s in (15, 17):
                            if s == 15:
                                e.wait_ge(hyout, L * 6 + 6)
                            c = (s - 15) // 2
                            e.activation(uH[:, 3 + c, :], yb[c][:], ACT.Copy).then_inc(ybh, 1)
                        if 8 <= s < 20 and s % 2 == 0:
                            if s == 8:
                                e.wait_ge(unit_done, L * UNITS + (U_WO + USED0))
                                e.wait_ge(evac, L * UNITS + (U_WO + EVAC0))
                                e.wait_ge(vt_mm, L * 9 + 9)
                            if s == 14:
                                e.wait_ge(biased, L * ITEMS + 6)
                            j = (s - 8) // 2
                            dst, src = (ac["kCh"], at["kC"]) if j < 3 else (ac["qCh"], at["qC"])
                            e.activation(dst[:, j % 3, :], src[:, j % 3, :], ACT.Copy).then_inc(c_high, 1)

            e.wait_ge(const_set, 1)
            load_log_exp()
            with e.Fori(0, LAYERS) as L:
                ffn(L, 0)
                high(e, L, U_HY, DT)
                high(e, L, U_HY + 1, DT)
                prenorm(L, 1, U_HY)
                pre_rs(L, 1)
                for j in range(2, 6):
                    high(e, L, U_HY + j + 2, DT)
                    if j < 5:
                        e.wait_ge(f_bias, L + 1)
                        e.wait_ge(f_mm, L * 3 + j - 1)
                        e.activation(tmp[1][0:FW, :], bank[4][0:FW, :], ACT.Identity, scale=hy["fv"][0:FW, 3:4],
                                     bias=hy["fv"][0:FW, 2 + j:3 + j]).then_inc(f_arg, 1)
                        e.wait_ge(f_red, L * 15 + 5 * j - 5)
                        e.activation(tmp[3][0:FW, :], tmp[1][0:FW, :], ACT.Sin).then_inc(f_sin, 1)
                    else:
                        load_log_exp()
                        e.wait_ge(hy_loaded, L * 48 + 48)
                        e.activation(tmp[0][:], tmp[0][:], ACT.Abs).then_inc(absd, 1)
                        e.wait_ge(absd, L + 1)
                        for m in range(4):
                            if m >= 2:
                                e.wait_ge(taps_ready, L * 7 + m - 1)
                            e.activation(tmp[1 + m % 2][:], tmp[0][:], ACT.Exp,
                                         scale=hy["tneg"][:, m:m + 1]).then_inc(window, 1)
                for n in range(2):
                    e.wait_ge(zt_mm, L * 2 + n + 1)
                    e.activation(hy["zt"][:, 2 * n:2 * n + 2, :], bank[4 + n][:].rearrange("p (k c) -> p k c", k=2),
                                 ACT.Copy).then_inc(zt_ready, 1)
                for n in range(4):
                    e.wait_ge(filt_mm, L * 4 + n + 1)
                    e.activation(hy["filt"][:, n // 2, n % 2 * 2:n % 2 * 2 + 2, :],
                                 bank[4 + n][:].rearrange("p (k c) -> p k c", k=2), ACT.Copy).then_inc(filt_ready, 1)
                for c in range(HYT):
                    e.wait_ge(hyout, L * 6 + 2 * c + 2)
                    e.activation(tmp[4 + c][:], yb[c][:], ACT.Square).then_inc(hysq, 1)
                e.wait_ge(hysum, L + 1)
                e.activation(rsp[:], bank[6][:], ACT.Ln, scale=1.0 / (HYT * P), bias=epsc[:, 0:1]).then_inc(hylog, 1)
                e.wait_ge(hylog, L + 1)
                e.activation(rsp[:], rsp[:], ACT.Exp, scale=-0.5).then_inc(hyrs, 1)
                for j in range(18):
                    if j < 16:
                        high(e, L, U_VA + j + 2, DT)
                    if 1 <= j <= 3:
                        for half in range(2):
                            e.wait_ge(vt_mm, L * 9 + 2 * (j - 1) + half + 1)
                            w = 4 - half
                            e.activation(at["VA"][:, 4 * half:4 * half + w, (j - 1) * P:j * P],
                                         bank[4 + half][:, 0:w * P].rearrange("p (n c) -> p n c", n=w),
                                         ACT.Copy).then_inc(vt_out, 1)
                    elif 4 <= j <= 6:
                        e.wait_ge(vt_mm, L * 9 + j + 3)
                        e.activation(at["VC"][:, :, (j - 4) * P:(j - 3) * P],
                                     bank[(4, 5, 4)[j - 4]][:].rearrange("p (n c) -> p n c", n=4),
                                     ACT.Copy).then_inc(vt_out, 1)
                    if j in (15, 16):
                        attention(L, "mixer", [j - 15])
                attention(L, "mixer", range(2, 55))
                def out_tiles(base, a):
                    for j in range(8):
                        if j < 6:
                            high(e, L, base + j + 2, DT)
                        else:
                            wait_unit(e, L, base + j)
                        y_tile(L, a, j, bank[(base + j) % 4], xa["yx"][:, j, :], 1)
                    post_rs(L, a)
                out_tiles(U_WO, 1)
                high(e, L, U_XQ, DT)
                high(e, L, U_XQ + 1, DT)
                prenorm(L, 2, U_XQ)
                pre_rs(L, 2)
                for j in range(24):
                    if 2 <= j < 22:
                        high(e, L, U_XQ + j + 2, DT)
                    if j == 0:
                        e.wait_ge(mem_loaded, L * 16 + 16)
                    if j < 8:
                        e.activation(xa["memH"][:, j, :], xa["memT"][:, j, :], ACT.Copy,
                                     scale=pr[:, G0 + G_MEM * 8 + j:G0 + G_MEM * 8 + j + 1]).then_inc(memh_ready, 1)
                    if j < 4:
                        if j >= 2:
                            e.wait_ge(s_msq, L * 16 + 4 * j - 4)
                        e.activation(tmp[4 + j % 2][:].rearrange("p (k m) -> p k m", k=2),
                                     xa["memT"][:, 2 * j:2 * j + 2, :], ACT.Square).then_inc(s_mact, 1)
                    if j == 5:
                        e.wait_ge(s_mmm, L + 1)
                        e.activation(rsm[:], bank[7][:, 0:MT], ACT.Ln, scale=1.0 / D,
                                     bias=epsc[:, 0:1]).then_inc(mem_log, 1)
                        e.wait_ge(mem_log, L + 1)
                        e.activation(rsm[:], rsm[:], ACT.Exp, scale=-0.5).then_inc(rsm_ready, 1)
                    if j >= 17 and j % 2 == 1:
                        n = (j - 17) // 2
                        e.wait_ge(kt_mm, L * 4 + n + 1)
                        e.activation(xa["kX"][:, 2 * n:2 * n + 2, :],
                                     bank[4 + n % 2][:].rearrange("p (c m) -> p c m", c=2),
                                     ACT.Copy).then_inc(kt_out, 1)
                high(e, L, U_XO, DT)
                high(e, L, U_XO + 1, DT)
                attention(L, "cross", range(22))
                out_tiles(U_XO, 2)
                high(e, L, U_IN[1], DT)
                high(e, L, U_IN[1] + 1, DT)
                prenorm(L, 3, U_IN[1])
                ffn(L, 1)

        @block.vector
        def _(e):
            def update(L, a, k, y):
                t = tmp[1 + k % 2]
                e.scalar_tensor_tensor(t[:], y[:, k, :], pr[:, G0 + POST[a] * 8 + k:G0 + POST[a] * 8 + k + 1],
                                       rsp[:], ALU.mult, ALU.mult).then_inc(y_scaled, 1)
                e.wait_ge(y_scaled, L * 32 + (a * 8 + k + 1))
                e.tensor_tensor(xT[:, k, :], xT[:, k, :], t[:], ALU.add).then_inc(x_ready, 1)

            def low_u(L, a, k):
                e.wait_ge(uh_ready, L * 32 + (a * 8 + k + 1))
                e.scalar_tensor_tensor(uL[:, k, :], xT[:, k, :], pr[:, G0 + PRE[a] * 8 + k:G0 + PRE[a] * 8 + k + 1],
                                       uH[:, k, :].bitcast(F32), ALU.mult, ALU.subtract).then_inc(u_ready, 1)

            def post_rs(L, a):
                e.wait_ge(rsp_ready, L * 4 + (a + 1))

            def pre_rs(L, a):
                wait_apart(e, rs_ready, L * 4 + (a + 1))

            def add_pre(L, a, u):
                for k in range(DT):
                    n = L * 32 + (a * 8 + k)
                    e.wait_ge(presq, n + 1)
                    if k == 0:
                        e.tensor_copy(tmp[3][:], tmp[4][:]).then_inc(preacc, 1)
                    else:
                        e.wait_ge(preacc, n)
                        e.tensor_tensor(tmp[3][:], tmp[3][:], tmp[4 + k % 2][:], ALU.add).then_inc(preacc, 1)
                    if k == 1:
                        low(e, L, u + 2, DT)
                low(e, L, u + 3, DT)

            def boundary(L, a, y, u):
                post_rs(L, a)
                for k in range(DT + 1):
                    if k < DT:
                        update(L, a, k, y)
                    if k >= 1:
                        e.wait_ge(x_ready, L * 32 + (a * 8 + k + X0))
                        low_u(L, a + 1, k - 1)
                add_pre(L, a + 1, u)
                pre_rs(L, a + 1)

            def add_square(L, a, j, it=0):
                n = L * 32 + 2 * it + (a * 8 + j)
                e.wait_ge(postsq, n + 1)
                if j == 0 and isinstance(it, int) and it == 0:
                    e.tensor_copy(tmp[0][:], tmp[4][:]).then_inc(postacc, 1)
                else:
                    e.wait_ge(postacc, n)
                    e.tensor_tensor(tmp[0][:], tmp[0][:], tmp[4 + j % 2][:], ALU.add).then_inc(postacc, 1)

            def ffn(L, f):
                a = 3 * f
                if f == 0:
                    e.wait_ge(params_loaded, L * 16 + 16)
                    e.wait_ge(x_ready, L * 32 + X0)
                    low(e, L, U_IN[0], DT)
                    low(e, L, U_IN[0] + 1, DT)
                    for k in range(DT):
                        low_u(L, 0, k)
                    add_pre(L, 0, U_IN[0])
                    pre_rs(L, 0)

                def pair(q, it, ahead):
                    p = L * 44 + 2 * it + (f * 22 + q)
                    u = U_IN[f] + 2 * q
                    n = L * UNITS + 4 * it
                    e.wait_ge(unit_done, n + (u + 1 + USED0))
                    e.tensor_tensor(tmp[q][:], bank[u % 4][:], rs[:], ALU.mult).then_inc(gate_scaled, 1)
                    if ahead:
                        low(e, L, u + 2, DT, it)
                    e.wait_ge(unit_done, n + (u + 2 + USED0))
                    e.tensor_tensor(tmp[2 + q][:], bank[u % 4 + 1][:], rs[:], ALU.mult).then_inc(evac, 2)
                    if ahead:
                        low(e, L, u + 3, DT, it)
                    e.wait_ge(evac, n + (u + 2 + EVAC0))
                    e.wait_ge(silu_ready, p + 1)
                    e.tensor_tensor(tmp[2 + q][:], tmp[q][:], tmp[2 + q][:], ALU.mult).then_inc(hid_ready, 1)
                    e.wait_ge(hidh_ready, p + 1)
                    at_ = bass.ds((2 * it + q) * T, T)
                    e.tensor_tensor(hL[:, at_], tmp[2 + q][:], hH[:, at_].bitcast(F32),
                                    ALU.subtract).then_inc(hid_split, 1)
                pair(0, 0, False)
                pair(1, 0, True)
                with e.Fori(1, FT // 2 - 1) as it:
                    pair(0, it, True)
                    pair(1, it, True)
                last = FT // 2 - 1
                pair(0, last, True)
                low(e, L, U_OUT[f], FH)
                pair(1, last, False)
                low(e, L, U_OUT[f] + 1, FH)

                def tile(q, it, ahead):
                    u = U_OUT[f] + 2 * q
                    if ahead:
                        low(e, L, u + 2, FH, it)
                        low(e, L, u + 3, FH, it)
                    add_square(L, a, q, it)
                tile(0, 0, True)
                tile(1, 0, True)
                with e.Fori(1, 3) as it:
                    tile(0, it, True)
                    tile(1, it, True)
                tile(0, 3, True)
                tile(1, 3, False)

            def attention(L, part, steps):
                first, n, g0 = (IT_A, 48, GR_A) if part == "mixer" else (IT_X, 16, GR_X)
                per = 2 if part == "cross" else 6
                turn = 5 if part == "cross" else 6
                w = 256 if part == "cross" else 64
                for s in steps:
                    if s < n:
                        t = first + s
                        kind = kind_of(t)
                        i, h = (t // 6 % 4, t % 6)
                        wait_apart(e, score_mm, L * ITEMS + (t + 1))
                        S = bank[t % 2]
                        if kind == "C" and t == IT_C:
                            e.wait_ge(c_strip_loaded, L * 16 + 16)
                        if kind == "X":
                            e.tensor_reduce(negmax[:, t:t + 1], S[:, 0:MEM], AX.X, ALU.min).then_inc(biased, 1)
                        else:
                            if s >= 4:
                                wait_apart(e, pt_mm, L * ITEMS + (t - 3))
                            if kind == "A":
                                width, bias = 256, at["biasA"][:, (0, 1, 1, 2)[i], h, :]
                            else:
                                width, bias = 512, strip[:, h, (3 - i) * P:(3 - i) * P + T]
                            e.tensor_tensor_reduce(tmp[t % 4][:, 0:width], S[:, 0:width], bias, 1.0, 3.0e38,
                                                   ALU.add, ALU.min, negmax[:, t:t + 1]).then_inc(biased, 1)
                    s3 = s - 3
                    if 0 <= s3 < n and s3 % per == per - 1:
                        g = g0 + s3 // per
                        t = first + s3
                        lo = t - per + 1
                        e.wait_ge(prob_ready, L * ITEMS + (t + 1))
                        e.reciprocal(rden[:, lo:t + 1], den[:, lo:t + 1]).then_inc(rden_ready, 1)
                        e.wait_ge(rden_ready, L * GROUPS + (g + 1))
                        e.wait_ge(pv_mm, L * ITEMS + (t + 1))
                        if s3 // per >= 1:
                            e.wait_ge(ot_mm, L * GROUPS + g)
                        last = e.tensor_tensor(
                            on[:, 0:per * w].rearrange("p (h c) -> p h c", h=per),
                            bank[4 + g % 2][:, 0:per * w].rearrange("p (h c) -> p h c", h=per),
                            rden[:, lo:t + 1].unsqueeze(2).to_broadcast([P, per, w]), ALU.mult)
                        last.then_inc(o_read, 1)
                        e.wait_ge(o_read, L * GROUPS + (g + 1))
                        if part == "mixer":
                            e.tensor_tensor_reduce(yx_free(L)[:, 0:384], on[:, 0:384], on[:, 0:384], 1.0, 0.0,
                                                   ALU.mult, ALU.add, gss[:, 0, g:g + 1]).then_inc(g_sq, 1)
                        else:
                            e.sem_inc(o_ready, 1)
                    s5 = s - 5
                    if part == "mixer" and 0 <= s5 < n and s5 % per == per - 1:
                        g = g0 + s5 // per
                        e.wait_ge(g_rs, L * 8 + (g + 1))
                        e.tensor_scalar(on[:, 0:384], on[:, 0:384], gss[:, 2, g:g + 1], None,
                                        ALU.mult).then_inc(o_ready, 1)
                    s5 = s - turn - (part == "mixer")
                    if 0 <= s5 < n and s5 % per == per - 1:
                        g = g0 + s5 // per
                        b = bank[6 + g % 2]
                        kind = kind_of(first + s5)
                        if kind == "X":
                            e.wait_ge(oh_ready, L * 32 + (24 + g - GR_X + 1))
                            e.tensor_tensor(x_out(uL, g - GR_X), b[:].rearrange("p (c n) -> p c n", c=4),
                                            x_out(uH, g - GR_X).bitcast(F32), ALU.subtract).then_inc(o_split, 1)
                        else:
                            e.wait_ge(oh_ready, L * 32 + (3 * g + 3))
                            for c in range(3):
                                dst, src, k = ac_out(uL, kind, g % 4, c)
                                hi = ac_out(uH, kind, g % 4, c)[0].bitcast(F32)
                                e.scalar_tensor_tensor(dst, src(b),
                                                       pr[:, G0 + G_GROUP * 8 + k:G0 + G_GROUP * 8 + k + 1],
                                                       hi, ALU.mult, ALU.subtract).then_inc(o_split, 1)
                    if part == "mixer":
                        if s in (28, 32):
                            low(e, L, U_WO + (s - 28) // 4, DT)
                        if s in (18, 20):
                            c = (s - 18) // 2
                            e.wait_ge(ybh, L * 2 + c + 1)
                            e.tensor_tensor(uL[:, 3 + c, :], yb[c][:], uH[:, 3 + c, :].bitcast(F32),
                                            ALU.subtract).then_inc(m_ready, 1)
                        if 9 <= s < 21 and s % 2 == 1:
                            j = (s - 9) // 2
                            e.wait_ge(c_high, L * 6 + j + 1)
                            hi, lo_, src = (ac["kCh"], ac["kCl"], at["kC"]) if j < 3 else \
                                (ac["qCh"], ac["qCl"], at["qC"])
                            j = j % 3
                            e.tensor_tensor(lo_[:, j, :], src[:, j, :], hi[:, j, :].bitcast(F32),
                                            ALU.subtract).then_inc(c_split, 1)

            def yx_free(L):
                return rsq

            e.memset(ones[:], 1.0)
            e.memset(epsc[:, 0:1], EPS)
            e.memset(epsc[:, 1:2], 4 * EPS).then_inc(const_set, 1)
            e.sem_inc(split_ready, SPLIT0)
            e.sem_inc(evac, EVAC0)
            e.wait_ge(setup_loaded, 16 * 4)
            for c in range(2):
                e.wait_ge(s_t5, c + 1)
                e.tensor_tensor(st["lnn"][0:C_H, c * T:c * T + T], st["lnn"][0:C_H, c * T:c * T + T],
                                bank[c][0:C_H, :], ALU.subtract).then_inc(s_t5b, 1)
            e.wait_ge(x_loaded, 16 * DT)
            e.sem_inc(x_ready, X0)

            with e.Fori(0, LAYERS) as L:
                ffn(L, 0)
                low(e, L, U_HY, DT)
                low(e, L, U_HY + 1, DT)
                boundary(L, 0, yf, U_HY)
                e.memset(hy["p"][:, :, 0:1], 0.0)
                e.memset(hy["p"][:, :, T + 1:T + 2], 0.0).then_inc(pad_zero, 1)
                e.wait_ge(pad_zero, L + 1)
                fv = hy["fv"]
                e.wait_ge(hy_small, L * 112 + 112)
                e.tensor_scalar(fv[0:FW, 4:7], fv[0:FW, 0:3], fv[0:FW, 3:4], None, ALU.mult).then_inc(f_bias, 1)
                for j in range(6):
                    if j >= 2:
                        low(e, L, U_HY + j + 2, DT)
                    wait_unit(e, L, U_HY + j)
                    p = hy["p"]
                    c = hy["uc"][:, j, :]
                    cw = [pr[:, CW0 + 6 * n + j:CW0 + 6 * n + j + 1] for n in range(3)]
                    e.tensor_tensor(p[:, j, 1:T + 1], bank[(U_HY + j) % 4][:], rs[:], ALU.mult).then_inc(evac, 1)
                    e.wait_ge(evac, L * UNITS + (U_HY + j + 1 + EVAC0))
                    e.tensor_scalar(c, p[:, j, 0:T], cw[0], pr[:, CB0 + j:CB0 + j + 1], ALU.mult,
                                    ALU.add).then_inc(conv, 1)
                    for n in (1, 2):
                        e.wait_ge(conv, L * 18 + (3 * j + n))
                        e.scalar_tensor_tensor(c, p[:, j, n:n + T], cw[n], c, ALU.mult, ALU.add).then_inc(conv, 1)
                    if j == 3:
                        for n in range(HYT):
                            e.wait_ge(conv, L * 18 + 12)
                            e.tensor_tensor(hy["uc"][:, n, :], hy["uc"][:, 2 + n, :], hy["uc"][:, n, :],
                                            ALU.mult).then_inc(z_ready, 1)
                    if 2 <= j < 5:
                        a, n = tmp[1][0:FW, :], tmp[2][0:FW, :]
                        r = L * 15 + 5 * (j - 2)
                        e.wait_ge(f_arg, L * 3 + j - 1)
                        e.tensor_scalar(n, a, 1 / (2 * math.pi), ROUND, ALU.mult, ALU.add).then_inc(f_red, 1)
                        e.wait_ge(f_red, r + 1)
                        e.tensor_scalar(n, n, ROUND, None, ALU.subtract).then_inc(f_red, 1)
                        e.wait_ge(f_red, r + 2)
                        e.scalar_tensor_tensor(a, n, -TWO_PI_HI, a, ALU.mult, ALU.add).then_inc(f_red, 1)
                        e.wait_ge(f_red, r + 3)
                        e.scalar_tensor_tensor(a, n, -TWO_PI_LO, a, ALU.mult, ALU.add).then_inc(f_red, 1)
                        e.wait_ge(f_red, r + 4)
                        e.tensor_scalar(a, a, -PI_IN, PI_IN, ALU.max, ALU.min).then_inc(f_red, 1)
                    if j == 5:
                        for m in range(4):
                            e.wait_ge(window, L * 4 + m + 1)
                            e.wait_ge(taps_mm, L * 4 + m + 1)
                            e.tensor_tensor(hy["taps"][:, m, :], bank[4 + m][:], tmp[1 + m % 2][:],
                                            ALU.mult).then_inc(taps_ready, 1)
                        e.wait_ge(taps_ready, L * 7 + 4)
                        e.memset(hy["taps"][0:1, 0, 256:512], 0.0).then_inc(taps_ready, 1)
                        e.wait_ge(taps_ready, L * 7 + 5)
                        e.tensor_tensor(hy["even"][:], hy["taps"][:, :, 0:256], hy["taps"][:, :, 256:512],
                                        ALU.add).then_inc(taps_ready, 1)
                        e.tensor_tensor(hy["taps"][:, :, 256:512], hy["taps"][:, :, 256:512],
                                        hy["taps"][:, :, 0:256], ALU.subtract).then_inc(taps_ready, 1)
                e.wait_ge(filt_ready, L * 4 + 4)
                e.wait_ge(z_mm, L * 4 + 4)
                for half in range(2):
                    ks = slice(2 * half, 2 * half + 2)
                    zc = bank[6 + half][:].rearrange("p (k c) -> p k c", k=2)
                    zs = bank[4 + half][:].rearrange("p (k c) -> p k c", k=2)
                    fe, fo = hy["filt"][:, 0, ks, :], hy["filt"][:, 1, ks, :]
                    yr, yn, t = hy["taps"][:, ks, 0:256], hy["taps"][:, ks, 256:512], hy["even"][:, ks, :]
                    r = L * 12 + 6 * half
                    e.tensor_tensor(yr, zc, fe, ALU.mult).then_inc(prod, 1)
                    e.tensor_tensor(t, zs, fo, ALU.mult).then_inc(prod, 1)
                    e.wait_ge(prod, r + 2)
                    e.tensor_tensor(yr, yr, t, ALU.add).then_inc(prod, 1)
                    e.tensor_tensor(yn, zs, fe, ALU.mult).then_inc(prod, 1)
                    e.wait_ge(prod, r + 3)
                    e.tensor_tensor(t, zc, fo, ALU.mult).then_inc(prod, 1)
                    e.wait_ge(prod, r + 5)
                    e.tensor_tensor(yn, yn, t, ALU.subtract).then_inc(prod, 1)
                for c in range(HYT):
                    e.wait_ge(y_mm, L * 2 + c + 1)
                    e.wait_ge(z_ready, L * 2 + 2)
                    e.scalar_tensor_tensor(yb[c][:], hy["uc"][:, c, :], pr[:, SK0 + c:SK0 + c + 1],
                                           bank[4 + c][:], ALU.mult, ALU.add).then_inc(hyout, 1)
                    e.wait_ge(conv, L * 18 + 18)
                    e.wait_ge(hyout, L * 6 + 2 * c + 1)
                    e.tensor_tensor(yb[c][:], yb[c][:], hy["uc"][:, 4 + c, :], ALU.mult).then_inc(hyout, 1)
                e.wait_ge(hyrs, L + 1)
                for c in range(HYT):
                    e.scalar_tensor_tensor(yb[c][:], yb[c][:], pr[:, G0 + G_GROUP * 8 + 3 + c:G0 + G_GROUP * 8 + 4 + c],
                                           rsp[:], ALU.mult, ALU.mult).then_inc(hyout, 1)
                e.tensor_scalar(rsq[:], rs[:], -0.125, None, ALU.mult).then_inc(rsq_ready, 1)
                e.wait_ge(rsq_ready, L + 1)
                for j in range(18):
                    if j < 16:
                        low(e, L, U_VA + j + 2, DT)
                    wait_unit(e, L, U_VA + j)
                    b = bank[(U_VA + j) % 4]
                    if j < 6:
                        if j >= 3:
                            e.wait_ge(vt_mm, L * 9 + 2 * (j - 3) + 2)
                        dst = at["vt"][:, j % 3, :]
                        if j < 3:
                            e.tensor_tensor(by_column(dst), by_row(b[:]), by_row(rs[:]), ALU.mult).then_inc(evac, 1)
                        else:
                            e.tensor_tensor(dst, b[:], rs[:], ALU.mult).then_inc(evac, 1)
                    elif j < 9:
                        def grid(ap):
                            return ap.rearrange("p (r i c) -> p i r c", r=ROWS, i=4)
                        back = at["qA"][:, j - 6, ::-1].rearrange("p (i r c) -> p i r c", i=4, r=ROWS)[:, ::-1]
                        e.tensor_tensor(back, grid(b[:]), grid(rsq[:]), ALU.mult).then_inc(evac, 1)
                    elif j < 12:
                        e.tensor_tensor(by_column(at["kA"][:, j - 9, :]), by_row(b[:]), by_row(rs[:]),
                                        ALU.mult).then_inc(evac, 1)
                    elif j < 15:
                        back = at["qC"][:, j - 12, ::-1].rearrange("p (i n) -> p i n", i=4)[:, ::-1]
                        e.tensor_tensor(back, b[:].rearrange("p (i n) -> p i n", i=4),
                                        rsq[:].rearrange("p (i n) -> p i n", i=4), ALU.mult).then_inc(evac, 1)
                    else:
                        e.tensor_tensor(at["kC"][:, j - 15, :], b[:], rs[:], ALU.mult).then_inc(evac, 1)
                    if j == 15:
                        e.wait_ge(bias_ready, L * 18 + 18)
                    if j in (15, 16):
                        attention(L, "mixer", [j - 15])
                attention(L, "mixer", range(2, 56))

                def out_tiles(base, a):
                    for j in range(8):
                        if j < 6:
                            low(e, L, base + j + 2, DT)
                        add_square(L, a, j)
                out_tiles(U_WO, 1)
                low(e, L, U_XQ, DT)
                low(e, L, U_XQ + 1, DT)
                boundary(L, 1, xa["yx"], U_XQ)
                for j in range(24):
                    if 2 <= j < 22:
                        low(e, L, U_XQ + j + 2, DT)
                    if j < 8:
                        e.wait_ge(memh_ready, L * 8 + j + 1)
                        e.scalar_tensor_tensor(xa["memL"][:, j, :], xa["memT"][:, j, :],
                                               pr[:, G0 + G_MEM * 8 + j:G0 + G_MEM * 8 + j + 1],
                                               xa["memH"][:, j, :].bitcast(F32), ALU.mult,
                                               ALU.subtract).then_inc(mem_ready, 1)
                    if j < 4:
                        for n in range(2):
                            c = 2 * j + n
                            sq = tmp[4 + j % 2][:, n * MEM:n * MEM + MEM]
                            e.wait_ge(s_mact, L * 4 + j + 1)
                            if c == 0:
                                e.tensor_copy(tmp[2][:, 0:MEM], sq).then_inc(s_msq, 2)
                            else:
                                e.wait_ge(s_msq, L * 16 + 2 * c)
                                e.tensor_tensor(tmp[2][:, 0:MEM], tmp[2][:, 0:MEM], sq, ALU.add).then_inc(s_msq, 2)
                    if j < 8:
                        wait_unit(e, L, U_XQ + j)
                        e.scalar_tensor_tensor(xa["qX"][:, j, :], bank[(U_XQ + j) % 4][:], -1.0 / 16, rs[:],
                                               ALU.mult, ALU.mult).then_inc(evac, 1)
                    elif j % 4 == 3:
                        block = (j - 8) // 4
                        dst = xa["kT"] if block < 2 else xa["VX"]
                        wait_unit(e, L, U_XQ + j)
                        if block == 0:
                            wait_apart(e, rsm_ready, L + 1)
                        for m in range(MT):
                            e.tensor_scalar(dst[:, m, block % 2 * KVW:(block % 2 + 1) * KVW],
                                            bank[2 * (block % 2) + m][:], rsm[:, m:m + 1], None,
                                            ALU.mult).then_inc(evac, 2)
                low(e, L, U_XO, DT)
                low(e, L, U_XO + 1, DT)
                attention(L, "cross", range(22))
                out_tiles(U_XO, 2)
                low(e, L, U_IN[1], DT)
                low(e, L, U_IN[1] + 1, DT)
                boundary(L, 2, xa["yx"], U_IN[1])
                ffn(L, 1)
                post_rs(L, 3)
                for k in range(DT):
                    if k >= 2:
                        e.wait_ge(x_ready, L * 32 + (24 + k - 1 + X0))
                    update(L, 3, k, yf)

        @block.gpsimd
        def _(e):
            e.dma_start(st["hot"][0:32, :], k_hot).then_inc(setup_loaded, 16)
            e.dma_start(st["lnn"][0:C_H, :], k_lnn).then_inc(setup_loaded, 16)
            e.dma_start(st["t5s"][0:32, 0:C_H], t5).then_inc(setup_loaded, 16)
            e.dma_start(eye[:], k_eye).then_inc(setup_loaded, 16)
            e.wait_ge(s_t5b, 2)
            e.dma_start(scratch, st["lnn"][0:C_H, :]).then_inc(scratch_out, 16)
            e.wait_ge(scratch_out, 16)
            with e.Fori(0, LAYERS) as L:
                one = bass.ds(L, 1)
                wait_apart(e, x_ready, L * 32 + X0)
                e.dma_start(pr[:], par[one].rearrange("a p n -> (a p) n")).then_inc(params_loaded, 16)
                small = [(hy["fv"][0:FW, 0:4], fvec[one].rearrange("a p n -> (a p) n")),
                         (hy["w1"][0:EMB, :], fw1[one].rearrange("a p n -> (a p) n")),
                         (hy["emb"][0:EMB, :], k_emb),
                         (hy["w2"][0:FW, :], fw23[bass.ds(2 * L, 1)].rearrange("a p n -> (a p) n")),
                         (hy["w3"][0:FW, :], fw23[bass.ds(2 * L + 1, 1)].rearrange("a p n -> (a p) n")),
                         (hy["w4"][0:FW, :], fw4[one].rearrange("a p n -> (a p) n")),
                         (hy["tneg"][:], k_time)]
                wait_apart(e, unit_done, L * UNITS + (U_HY + USED0))
                for dst, src in small:
                    e.dma_start(dst, src).then_inc(hy_small, 16)
                for part in range(2):
                    e.dma_start(hy["fwd"][:, part], k_fwd[part]).then_inc(hy_loaded, 16)
                wait_apart(e, preacc, L * 32 + 16)
                e.dma_start(tmp[0][:], decay[one].to_broadcast([P, 512])).then_inc(hy_loaded, 16)
                e.dma_start(hy["inv"][:], k_inv).then_inc(inv_loaded, 16)
                wait_apart(e, hyout, L * 6 + 4)
                e.dma_start(amask, k_namask).then_inc(strips_loaded, 16)
                for h in range(NA_H):
                    for r in range(WR):
                        e.dma_start(rstrip[r * 16:r * 16 + 16, h],
                                    bass.AP(tensor=rpb.tensor, offset=L * (NA_H * 960) + (h * 960 + r * 64),
                                            ap=[[1, 16], [64, WR], [1, 48]])).then_inc(strips_loaded, 16)
                e.wait_ge(strips_loaded, L * (16 * 49) + 16 * 49)
                for y, c0 in enumerate((16, 8, 0)):
                    for h in range(NA_H):
                        e.tensor_tensor(by_column(at["biasA"][:, y, h, :]), by_column(amask[:, y, :]),
                                        rstrip[:, h, :, c0:c0 + 32], ALU.subtract).then_inc(bias_ready, 1)
                wait_apart(e, bias_ready, L * 18 + 18)
                e.dma_start(strip[:], bass.AP(tensor=scratch.tensor, offset=0,
                                              ap=[[1, P], [1024, C_H], [1, STRIP]])).then_inc(c_strip_loaded, 16)
                wait_apart(e, o_split, L * 32 + 24)
                e.dma_start(xa["memT"][:], mem).then_inc(mem_loaded, 16)


def by_row(ap):
    return ap.rearrange("p (r c) -> p r c", r=ROWS)


def by_column(ap):
    return ap.rearrange("p (c r) -> p r c", r=ROWS)


def kind_of(t):
    return "A" if t < IT_C else "C" if t < IT_X else "X"


def chunks_of(t):
    return 4 if kind_of(t) == "C" else 2


def splits_before(g):
    return 3 * g if g <= GR_X else 24 + g - GR_X


def x_out(t, g):
    i, pair = g // 2, g % 2
    return t[:, 4 * pair:4 * pair + 4, i * P:i * P + P]


def ac_out(t, kind, i, c):
    k = c if kind == "A" else 5 + c
    if kind == "A":
        dst = t[:, k, :].rearrange("p (r i c) -> p r i c", r=ROWS, i=4)[:, :, i, :]
        return dst, lambda b: b[:, c * P:c * P + P][:, ::-1].rearrange("p (r c) -> p r c", r=ROWS), k
    return t[:, k, i * P:i * P + P], lambda b: b[:, c * P:c * P + P][:, ::-1], k


def t5_bucket(rel):
    half, exact = 16, 8
    n = np.abs(rel)
    far = exact + (np.log(np.maximum(n, 1) / exact) / math.log(1024 / exact) * (half - exact)).astype(np.int32)
    far = np.minimum(far, half - 1)
    return np.where(rel > 0, half, 0) + np.where(n < exact, n, far)


def constants():
    f = np.float32
    t = np.linspace(0.0, 1.0, T, dtype=f)
    bands = np.linspace(1e-4, 15, 16, dtype=f)
    ang = (f(2.0 * math.pi / T) * np.arange(T, dtype=f))[:, None] * bands[None, :]
    emb = np.concatenate([t[:, None], np.cos(ang), -np.sin(ang)], 1).astype(f).T.copy()
    kk = 2 * np.pi * (np.arange(T) + 0.5) / (2 * T)
    ph = np.outer(np.arange(T), kk)

    def tiles(a):
        return a.reshape(4, P, T).transpose(1, 0, 2)
    fwd = np.stack([tiles(np.cos(ph)), tiles(np.sin(ph))]).astype(f)
    inv = np.stack([tiles(np.cos(ph).T / T), tiles(np.sin(ph).T / T)], 1).astype(f)
    time = -t.reshape(4, P).T.copy()
    mask = np.full((3, P, 32, WR), BIG, f)
    for y, i in enumerate((0, 1, 3)):
        for c in range(16):
            col = 16 * i + c
            cs = min(max(col - WC // 2, 0), COLS - WC)
            keys = NA_START[i] + np.arange(32)
            ok = (keys >= cs) & (keys < cs + WC)
            for r in range(ROWS):
                mask[y, P - 1 - (r * 16 + c)][:] = np.where(ok[:, None], f(0), f(BIG))
    mask = mask.transpose(1, 0, 2, 3).reshape(P, 3, 256).copy()
    rel = np.arange(1023) - 511
    hot = np.zeros((32, 1024), f)
    hot[t5_bucket(rel), np.arange(1023)] = 1
    count = (np.abs(rel) <= 64).astype(int) + ((rel % 4 == 0) & (np.abs(rel) <= 256)) + (rel % 16 == 0)
    lnn = np.full(1024, BIG, f)
    lnn[:1023] = np.where(count > 0, -np.log(np.maximum(count, 1)), BIG)
    return dict(k_emb=emb, k_fwd=fwd, k_inv=inv, k_time=time, k_namask=mask, k_hot=hot,
                k_lnn=np.tile(lnn, (C_H, 1)), k_eye=np.eye(P, dtype=f))


def columns(w, k):
    lead = w.shape[:-2]
    n = w.shape[-1] // P
    w = w.reshape(*lead, k, P, n, P)
    m = len(lead)
    w = w.transpose(*range(m), m + 2, m + 1, m, m + 3)
    return w.reshape(*lead, n, P, k * P)


def lay_out(i):
    a = {}
    a["x"] = i["x"][0].T.reshape(DT, P, T)
    a["mem"] = i["mem"][0].T.reshape(DT, P, MEM).transpose(1, 0, 2)
    g = i["norm_g"].reshape(LAYERS, 10, DT, P).transpose(0, 3, 1, 2).reshape(LAYERS, P, 80)
    cw = i["hy_conv_w"].reshape(LAYERS, 3, 6, P).transpose(0, 3, 1, 2).reshape(LAYERS, P, 18)
    cb = i["hy_conv_b"].reshape(LAYERS, 6, P).transpose(0, 2, 1)
    sk = i["hy_skip"].reshape(LAYERS, HYT, P).transpose(0, 2, 1)
    a["par"] = np.concatenate([g, cw, cb, sk], -1)
    first = columns(i["ffn_w_in"], DT)
    first = first.reshape(LAYERS, 2, 2, FT, P, D).transpose(0, 1, 3, 2, 4, 5)
    a["w_first"] = first.reshape(LAYERS * 88, P, D)
    second = i["ffn_w_out"].reshape(LAYERS, 2, 2, FH, P, DT, P).transpose(0, 1, 5, 2, 4, 3, 6)
    a["w_second"] = second.reshape(LAYERS * 32, P, FH * P)
    w_in = columns(i["w_in"], DT)
    order = [9, 10, 11, 12, 13, 14, 6, 7, 8, 21, 22, 23, 0, 1, 2, 3, 4, 5, 15, 16, 17, 18, 19, 20]
    kv = i["xa_wkv"].reshape(LAYERS, DT // 2, 2, P, 2 * D // KVW, KVW).transpose(0, 4, 1, 3, 2, 5)
    kv = kv.reshape(LAYERS, 16, P, D)
    a["w_proj"] = np.concatenate([w_in[:, order], columns(i["w_out"], DT), columns(i["xa_wq"], DT), kv,
                                  columns(i["xa_wo"], DT)], 1
                                 ).reshape(LAYERS * 64, P, D)
    rpb = np.zeros((LAYERS, NA_H, 15, 64), i["na_rpb"].dtype)
    rpb[..., 16:47] = i["na_rpb"]
    a["rpb"] = rpb.reshape(-1)
    a["t5"] = i["t5_table"]
    a["fw1"] = i["hy_f_w1"]
    a["fw23"] = np.stack([i["hy_f_w2"], i["hy_f_w3"]], 1).reshape(LAYERS * 2, FW, FW)
    a["fw4"] = i["hy_f_w4"]
    a["fvec"] = np.stack([i["hy_f_b1"], i["hy_f_b2"], i["hy_f_b3"], i["hy_freq"]], -1)
    a["decay"] = i["hy_decay"]
    return a


ORDER = ("x", "mem", "par", "w_first", "w_second", "w_proj", "rpb", "t5", "fw1", "fw23", "fw4", "fvec", "decay",
         "k_emb", "k_fwd", "k_inv", "k_time", "k_namask", "k_hot", "k_lnn", "k_eye")


def kernel(**inputs):
    import concourse.bacc as bacc
    from concourse.bass_utils import run_bass_kernel_spmd

    nc = bacc.Bacc("TRN2", target_bir_lowering=False, num_devices=1)
    data = lay_out({k: np.asarray(v) for k, v in inputs.items()})
    data.update(constants())
    arrays, args = {}, []
    for name in ORDER:
        a = np.ascontiguousarray(data[name])
        arrays["in_" + name] = a
        args.append(nc.dram_tensor("in_" + name, a.shape, mybir.dt.from_np(a.dtype), kind="ExternalInput").ap())
    args.append(nc.dram_tensor("out_x", (DT, P, T), F32, kind="ExternalOutput").ap())
    build(nc, *args)
    got = run_bass_kernel_spmd(nc, [arrays], core_ids=[0])
    return np.ascontiguousarray(got.results[0]["out_x"].reshape(D, T).T[None])
```
